# Optimizing a Trainium2 kernel written in Bass

```python
import math
import jax
import jax.numpy as jnp
from jax import lax
import numpy as np

D_MODEL = 2048
BATCH = 1
SEQ = 256
DEPTH = 1
DEC_BATCH = 8
DEC_SEQ = 4
PAST_LEN = 256
PAGE_SIZE = 128

N_HEADS = 16
N_KV_HEADS = 4
D_HEAD = 64
ATTN_W = N_HEADS * D_HEAD
KV_W = N_KV_HEADS * D_HEAD
IDX_HEADS = 8
D_IDX = 64
TOPK_MAX = 256
Q_BLOCK = 128
S5_W = D_MODEL // 2
S5_GROUP = 16
S5_GROUPS = S5_W // S5_GROUP
S5_STATE = 64
STEP_MIN = 0.001
STEP_MAX = 0.1
D_FF = 11 * D_MODEL // 4
CONV_W = 3
EPS = 1e-6
IN_SPLITS = (ATTN_W, KV_W, KV_W, IDX_HEADS * D_IDX, D_IDX, IDX_HEADS, S5_W, D_MODEL, D_MODEL)
IN_COLS = sum(IN_SPLITS)

kernel_name = "hybrid_dsa_s5_convffn_step"

def _rmsnorm(x, g):
    xf = x.astype(jnp.float32)
    y = xf * lax.rsqrt(jnp.mean(xf * xf, axis=-1, keepdims=True) + EPS) * g.astype(jnp.float32)
    return y.astype(x.dtype)

def _dsa_block(q, qi, wi, qpos, k, v, ki, kpos):
    b, t = q.shape[0], q.shape[1]
    k_sel = min(TOPK_MAX, k.shape[1] // 4)
    logits = jax.nn.relu(jnp.einsum('bthd,bsd->btsh', qi.astype(jnp.float32), ki.astype(jnp.float32)) * (D_IDX ** -0.5))
    score = jnp.einsum('btsh,bth->bts', logits, wi.astype(jnp.float32) * (IDX_HEADS ** -0.5))
    causal = kpos[None, :] <= qpos[:, None]
    score = jnp.where(causal[None], score, -jnp.inf)
    _, idx = lax.top_k(score, k_sel)
    valid = kpos[idx] <= qpos[None, :, None]
    gather = jax.vmap(lambda rows, ii: rows[ii])
    k_g = gather(k, idx).astype(jnp.float32)
    v_g = gather(v, idx).astype(jnp.float32)
    qg = q.reshape(b, t, N_KV_HEADS, N_HEADS // N_KV_HEADS, D_HEAD).astype(jnp.float32)
    s = jnp.einsum('btngd,btjnd->btngj', qg, k_g) * (D_HEAD ** -0.5)
    s = jnp.where(valid[:, :, None, None, :], s, -jnp.inf)
    p = jax.nn.softmax(s, axis=-1)
    o = jnp.einsum('btngj,btjnd->btngd', p, v_g)
    return o.reshape(b, t, ATTN_W).astype(q.dtype)

def _dsa_attend(q, qi, wi, qpos, k, v, ki, kpos):
    b, t = q.shape[0], q.shape[1]
    if t > Q_BLOCK and t % Q_BLOCK == 0:
        nb = t // Q_BLOCK

        def blocks(a):
            return jnp.moveaxis(a.reshape(b, nb, Q_BLOCK, *a.shape[2:]), 1, 0)

        out = lax.map(lambda args: _dsa_block(*args, k, v, ki, kpos),
                      (blocks(q), blocks(qi), blocks(wi), qpos.reshape(nb, Q_BLOCK)))
        return jnp.moveaxis(out, 0, 1).reshape(b, t, ATTN_W)
    return _dsa_block(q, qi, wi, qpos, k, v, ki, kpos)

def _lin_combine(left, right):
    a1, b1 = left
    a2, b2 = right
    return a2 * a1, a2 * b1 + b2

def _s5(u, x0_re, x0_im, a_re, a_im, log_step, b_re, b_im, c_re, c_im, d_skip):
    b, t = u.shape[0], u.shape[1]
    f32 = jnp.float32
    uf = u.astype(f32).reshape(b, t, S5_GROUPS, S5_GROUP)
    lam = lax.complex(a_re.astype(f32), a_im.astype(f32))
    step = jnp.exp(log_step.astype(f32))[:, None]
    lam_bar = jnp.exp(lam * step)
    b_bar = ((lam_bar - 1.0) / lam)[..., None] * lax.complex(b_re.astype(f32), b_im.astype(f32))
    bu = jnp.einsum('gpc,btgc->btgp', b_bar, uf.astype(jnp.complex64))
    x0 = lax.complex(x0_re.astype(f32), x0_im.astype(f32))
    bu = bu.at[:, 0].add(lam_bar[None] * x0)
    decay = jnp.broadcast_to(lam_bar, bu.shape)
    _, xs = lax.associative_scan(_lin_combine, (decay, bu), axis=1)
    c = lax.complex(c_re.astype(f32), c_im.astype(f32))
    y = jnp.real(jnp.einsum('gcp,btgp->btgc', c, xs)) + d_skip.astype(f32).reshape(S5_GROUPS, S5_GROUP) * uf
    last = xs[:, -1]
    return y.reshape(b, t, S5_W), jnp.real(last), jnp.imag(last)

def _conv_ffn(h, conv_state, w_up, conv_w, conv_b, w_down):
    t = h.shape[1]
    up = h @ w_up
    padded = jnp.concatenate([conv_state.astype(up.dtype), up], axis=1)
    mixed = conv_b
    for j in range(CONV_W):
        mixed = mixed + conv_w[j] * padded[:, j:j + t]
    gate, val = jnp.split(mixed, 2, axis=-1)
    out = (jax.nn.silu(gate) * val) @ w_down
    return out, padded[:, t:]

def _split_points():
    pts, acc = [], 0
    for w in IN_SPLITS[:-1]:
        acc += w
        pts.append(acc)
    return pts

def _layer(x, k_past, v_past, ki_past, s_re, s_im, conv_state, lp):
    (norm_mix, w_in, w_attn_proj, a_re, a_im, log_step, b_re, b_im, c_re, c_im, d_skip,
     w_glu, w_out, norm_ffn, w_up, conv_w, conv_b, w_down) = lp
    b, t = x.shape[0], x.shape[1]
    h = _rmsnorm(x, norm_mix)
    proj = h @ w_in
    q, k, v, qi, ki, wi, u, ga, gb = jnp.split(proj, _split_points(), axis=-1)
    q = q.reshape(b, t, N_HEADS, D_HEAD)
    k = k.reshape(b, t, N_KV_HEADS, D_HEAD)
    v = v.reshape(b, t, N_KV_HEADS, D_HEAD)
    qi = qi.reshape(b, t, IDX_HEADS, D_IDX)
    past = k_past.shape[1]
    k_all = jnp.concatenate([k_past.astype(k.dtype), k], axis=1)
    v_all = jnp.concatenate([v_past.astype(v.dtype), v], axis=1)
    ki_all = jnp.concatenate([ki_past.astype(ki.dtype), ki], axis=1)
    kpos = jnp.arange(past + t, dtype=jnp.int32)
    qpos = past + jnp.arange(t, dtype=jnp.int32)
    attn = _dsa_attend(q, qi, wi, qpos, k_all, v_all, ki_all, kpos)
    y_a = attn @ w_attn_proj
    s5_y, new_re, new_im = _s5(u, s_re, s_im, a_re, a_im, log_step, b_re, b_im, c_re, c_im, d_skip)
    z = jax.nn.gelu(s5_y).astype(x.dtype)
    glu_a, glu_g = jnp.split(z @ w_glu, 2, axis=-1)
    y_b = glu_a * jax.nn.sigmoid(glu_g)
    merged = jax.nn.sigmoid(ga) * y_a + jax.nn.sigmoid(gb) * y_b
    x = x + merged @ w_out
    ffn, new_conv = _conv_ffn(_rmsnorm(x, norm_ffn), conv_state, w_up, conv_w, conv_b, w_down)
    x = x + ffn
    return x, k, v, ki, new_re, new_im, new_conv

def setup_inputs(seed: int = 0) -> dict:
    key = jax.random.key(seed)
    ks = iter(jax.random.split(key, 40))
    f32 = jnp.float32

    def nrm(shape, scale):
        return jax.random.normal(next(ks), shape, f32) * scale

    n_pages = PAST_LEN // PAGE_SIZE
    n_pool = (DEC_BATCH * n_pages * 5) // 4
    page_table = jax.random.permutation(next(ks), n_pool)[:DEC_BATCH * n_pages].reshape(DEC_BATCH, n_pages).astype(jnp.int32)
    a_im_init = jnp.pi * jnp.arange(S5_STATE, dtype=f32)
    inp = {
        "x_prompt": nrm((BATCH, SEQ, D_MODEL), 1.0),
        "x_sample": nrm((DEC_BATCH, DEC_SEQ, D_MODEL), 1.0),
        "cache_k": nrm((DEPTH, n_pool, PAGE_SIZE, N_KV_HEADS, D_HEAD), 1.0),
        "cache_v": nrm((DEPTH, n_pool, PAGE_SIZE, N_KV_HEADS, D_HEAD), 1.0),
        "cache_kidx": nrm((DEPTH, n_pool, PAGE_SIZE, D_IDX), 1.0),
        "state_s5_re": nrm((DEPTH, DEC_BATCH, S5_GROUPS, S5_STATE), 0.3),
        "state_s5_im": nrm((DEPTH, DEC_BATCH, S5_GROUPS, S5_STATE), 0.3),
        "state_ffn_conv": nrm((DEPTH, DEC_BATCH, CONV_W - 1, 2 * D_FF), 1.0),
        "page_table": page_table,
        "norm_mix": 1.0 + nrm((DEPTH, D_MODEL), 0.02),
        "w_in": nrm((DEPTH, D_MODEL, IN_COLS), D_MODEL ** -0.5),
        "w_attn_proj": nrm((DEPTH, ATTN_W, D_MODEL), ATTN_W ** -0.5),
        "s5_a_re": -0.5 + nrm((DEPTH, S5_GROUPS, S5_STATE), 0.01),
        "s5_a_im": a_im_init + nrm((DEPTH, S5_GROUPS, S5_STATE), 0.01),
        "s5_log_step": jax.random.uniform(next(ks), (DEPTH, S5_GROUPS), f32, math.log(STEP_MIN), math.log(STEP_MAX)),
        "s5_b_re": nrm((DEPTH, S5_GROUPS, S5_STATE, S5_GROUP), (2 * S5_GROUP) ** -0.5),
        "s5_b_im": nrm((DEPTH, S5_GROUPS, S5_STATE, S5_GROUP), (2 * S5_GROUP) ** -0.5),
        "s5_c_re": nrm((DEPTH, S5_GROUPS, S5_GROUP, S5_STATE), (2 * S5_STATE) ** -0.5),
        "s5_c_im": nrm((DEPTH, S5_GROUPS, S5_GROUP, S5_STATE), (2 * S5_STATE) ** -0.5),
        "s5_d": nrm((DEPTH, S5_W), 1.0),
        "w_glu": nrm((DEPTH, S5_W, 2 * D_MODEL), S5_W ** -0.5),
        "w_out": nrm((DEPTH, D_MODEL, D_MODEL), D_MODEL ** -0.5),
        "norm_ffn": 1.0 + nrm((DEPTH, D_MODEL), 0.02),
        "w_up": nrm((DEPTH, D_MODEL, 2 * D_FF), D_MODEL ** -0.5),
        "conv_w": nrm((DEPTH, CONV_W, 2 * D_FF), CONV_W ** -0.5),
        "conv_b": nrm((DEPTH, 2 * D_FF), 0.02),
        "w_down": nrm((DEPTH, D_FF, D_MODEL), D_FF ** -0.5),
        "norm_final": 1.0 + nrm((D_MODEL,), 0.02),
    }
    return inp

def reference(x_prompt, x_sample, cache_k, cache_v, cache_kidx, state_s5_re, state_s5_im, state_ffn_conv,
              page_table, norm_mix, w_in, w_attn_proj, s5_a_re, s5_a_im, s5_log_step, s5_b_re, s5_b_im,
              s5_c_re, s5_c_im, s5_d, w_glu, w_out, norm_ffn, w_up, conv_w, conv_b, w_down, norm_final):
    xp, xs = x_prompt, x_sample
    bp, bs = xp.shape[0], xs.shape[0]
    kp_l, vp_l, kip_l, srp_l, sip_l, cp_l = [], [], [], [], [], []
    ks_l, vs_l, kis_l, srs_l, sis_l, cs_l = [], [], [], [], [], []
    for l in range(DEPTH):
        lp = (norm_mix[l], w_in[l], w_attn_proj[l], s5_a_re[l], s5_a_im[l], s5_log_step[l],
              s5_b_re[l], s5_b_im[l], s5_c_re[l], s5_c_im[l], s5_d[l], w_glu[l], w_out[l],
              norm_ffn[l], w_up[l], conv_w[l], conv_b[l], w_down[l])
        zk = jnp.zeros((bp, 0, N_KV_HEADS, D_HEAD), xp.dtype)
        zki = jnp.zeros((bp, 0, D_IDX), xp.dtype)
        zs = jnp.zeros((bp, S5_GROUPS, S5_STATE), jnp.float32)
        zc = jnp.zeros((bp, CONV_W - 1, 2 * D_FF), xp.dtype)
        xp, kp, vp, kip, srp, sip, cp = _layer(xp, zk, zk, zki, zs, zs, zc, lp)
        pk = cache_k[l][page_table].reshape(bs, -1, N_KV_HEADS, D_HEAD)
        pv = cache_v[l][page_table].reshape(bs, -1, N_KV_HEADS, D_HEAD)
        pki = cache_kidx[l][page_table].reshape(bs, -1, D_IDX)
        xs, ksm, vsm, kism, srs, sis, cs = _layer(xs, pk, pv, pki, state_s5_re[l], state_s5_im[l],
                                                 state_ffn_conv[l], lp)
        kp_l.append(kp); vp_l.append(vp); kip_l.append(kip); srp_l.append(srp); sip_l.append(sip); cp_l.append(cp)
        ks_l.append(ksm); vs_l.append(vsm); kis_l.append(kism); srs_l.append(srs); sis_l.append(sis); cs_l.append(cs)
    y_prompt = _rmsnorm(xp, norm_final)
    y_sample = _rmsnorm(xs, norm_final)
    return (y_prompt, y_sample,
            jnp.stack(kp_l), jnp.stack(vp_l), jnp.stack(kip_l), jnp.stack(srp_l), jnp.stack(sip_l), jnp.stack(cp_l),
            jnp.stack(ks_l), jnp.stack(vs_l), jnp.stack(kis_l), jnp.stack(srs_l), jnp.stack(sis_l), jnp.stack(cs_l))


_drawn_inputs = setup_inputs


def setup_inputs(seed=0):
    import zlib

    import numpy as np

    out = dict(_drawn_inputs(seed))
    spreads = {}
    factors = {'norm_mix': 2.727,
     's5_a_re': 4.421,
     'norm_ffn': 2.799,
     'conv_b': 3.922,
     'norm_final': 2.814}
    for name, (base, spread) in spreads.items():
        noise = np.random.default_rng([zlib.crc32(name.encode()), seed]).standard_normal(out[name].shape)
        drawn = base * np.exp(spread * noise) if base else spread * noise
        out[name] = jnp.asarray(drawn.astype(out[name].dtype))
    for name, factor in factors.items():
        out[name] = (out[name] * factor).astype(out[name].dtype)
    return out
```

```python
from contextlib import ExitStack

import concourse.bass as bass
from concourse import mybir

F32 = mybir.dt.float32
F32R = mybir.dt.float32r
BF16 = mybir.dt.bfloat16
I32 = mybir.dt.int32
ALU = mybir.AluOpType
ACT = mybir.ActivationFunctionType
AX_X = mybir.AxisListType.X
ds = bass.ds
ENGINES = {e.value: e for e in (mybir.EngineType.PE, mybir.EngineType.Activation, mybir.EngineType.DVE, mybir.EngineType.Pool, mybir.EngineType.SP)}

P = 128
D = 2048
KD = D // P
TP = 256
NB, DS = 8, 4
TS = NB * DS
T = TP + TS
PAGE, NPAGES, NPOOL = 128, 2, 20
PAST = PAGE * NPAGES
SK = PAST + DS
NKV, GQ, DH = 4, 4, 64
NPR = NKV // 2
IH, DI = 8, 64
KV = NKV * DH
GRP, GC, NST = 64, 16, 64
S5W = GRP * GC
NPAIR = GRP // 2
NUT = S5W // P
FF = 5632
KF = FF // P
EPS = 1e-6
NEG = -3.0e38
TOPK_ROUNDS = 8

CQ, CK, CV, CQI = 0, 1024, 1280, 1536
CKI, CWI, CU, CGA = 2048, 2112, 2120, 3144

KCH, CW, NSLOT = 4, 256, 4
KDN, NDN = 11, 2

C_U, C_KIWI, C_QI, C_KV, C_Q, C_GATE, C_GLU, C_PROJ, C_OUT, C_UP, C_END = 0, 16, 20, 28, 36, 52, 116, 148, 164, 196, 372
G_U, G_KIWI, G_QI, G_KV, G_Q, G_GATE, G_GLU, G_PROJ, G_OUT, G_UP, G_DOWN = 0, 4, 5, 7, 9, 13, 29, 45, 53, 61, 105
N_GATE, N_GLU, N_PROJ, N_OUT, N_UP, N_DOWN = 8, 8, 4, 4, 22, 4

TWO_PI = 6.283185307179586
PI1 = 6.28125
PI2 = 0.001934051513671875
PI3 = TWO_PI - PI1 - PI2
MAGIC = 12582912.0
LOG2E = 1.4426950408889634
LN2H = 0.693359375
LN2L = 0.6931471805599453 - LN2H
PI_IN = 3.1415925


def bc(ap, axis, n):
    a = ap.unsqueeze(axis)
    shape = list(a.shape)
    shape[axis] = n
    return a.broadcast_to(shape)


class Own:

    def __init__(self, eng, sem):
        self.eng, self.sem, self.n, self.off, self.start = eng, sem, 0, 0, 0

    def __call__(self, ins):
        ins.then_inc(self.sem, 1)
        self.n += 1

    def wait(self):
        self.eng.wait_ge(self.sem, self.off + self.n)

    def link(self, ins):
        self(ins)
        self.wait()

    def loop(self, step, per):
        self.start, self.off, self.per = self.n, step * per, per

    def done(self, turns):
        assert self.n - self.start == self.per, (self.n - self.start, self.per)
        self.n, self.off = self.start + self.per * turns, 0


def hybrid_decoder_step_kernel(nc, I, O, W):
    base = (nc.sbuf_base + 31) // 32 * 32

    def at(name, shape, dt, off):
        return nc.alloc_sbuf_tensor_at(name, shape, dt, offset=base + off)

    ident = at("ident", [P, P], F32, 0)
    ones = at("ones", [P, P], F32, 512)
    nvec = at("nvec", [P, 56], F32, 1024)
    convp = at("convp", [P, 4, 2 * KF], F32, 1248)
    rstd = at("rstd", [P, T], F32, 2656)
    sqacc = at("sqacc", [P, T], F32, 3808)
    nw = [at(f"newton{i}", [P, T], F32, 4960 + 1152 * i) for i in range(2)]
    rtok = at("rtok", [P, 8], F32, 7264)
    ptab = at("ptab", [1, NB * NPAGES], I32, 7296)
    GR = 7424
    RW = GR + 36864
    HL = RW + 16384
    RE = HL + 32768
    UZ, QT, KT, WK = RE + 36864, RE + 55296, RE + 64512, RE + 68864
    raw = at("raw", [P, NSLOT, KCH, CW], F32, RW)
    whi = at("whi", [P, NSLOT, KCH, CW], F32R, HL)
    wlo = at("wlo", [P, NSLOT, KCH, CW], F32R, HL + 16384)
    hhi = at("hhi", [P, KD, T], F32R, RE)
    hlo = at("hlo", [P, KD, T], F32R, RE + 18432)
    xt0 = at("xt0", [P, KD, T], F32, UZ)
    xin = at("xin", [P, 3, D], F32, WK)
    sqx = at("sqx", [P, D], F32, QT)
    uT = at("uT", [P, NUT, T], F32, UZ)
    zhi = at("zhi", [P, NUT, T], F32R, UZ)
    zlo = at("zlo", [P, NUT, T], F32R, UZ + 9216)
    vT = at("vT", [P, NPR, T], F32, UZ + 9216)
    ktok = at("ktok", [P, 3, KV], F32, UZ + 11520)
    vstok = at("vstok", [TS, KV], F32, UZ + 14592)
    kitok = at("kitok", [P, 3, DI], F32, UZ + 15616)
    qT = at("qT", [P, 8, T], F32, QT)
    kT = at("kT", [P, NPR, T], F32, KT)
    vtok = at("vtok", [P, 2, KV], F32, KT + 2304)
    nvn = at("nvn", [56, P], F32, KT)
    cvn = at("cvn", [2 * KF, 4, P], F32, KT + 512)
    apn = at("apn", [96, P], F32, KT + 2560)
    lsn = at("lsn", [96, 2], F32, KT + 3072)
    bdg = at("bdg", [P, 2, NPAIR, 32], F32, WK + 24576)
    cdg = at("cdg", [P, 2, NUT, P], F32, WK + 32768)
    bnat = at("bnat", [P, 2, NPAIR, GC], F32, WK + 40960)
    cnat = at("cnat", [P, 2, NUT, NST], F32, WK + 45056)
    stn = at("stn", [P, 2, 2, P], F32, 4960)
    lbt = at("lbt", [P, 2, NUT, P], F32, GR)
    cbt = at("cbt", [P, 2, NUT, P], F32, GR + 8192)
    tmp = [at(f"angle{i}", [P, NPAIR, 32], F32, GR + 4096 * i) for i in range(4)]
    x0 = at("x0", [P, 2, NB, NPAIR], F32, 4960)
    ang_hi = at("ang_hi", [P, NPAIR], BF16, 7360)
    e1 = at("e1", [P, NPAIR + 1, 2, 16], F32, GR + 16384)
    e1r = at("e1r", [P, NPAIR + 1, 2, 16], F32, GR + 20608)
    e2 = at("e2", [P, NPAIR + 1, 2, 16], F32, GR + 24832)
    inj = at("inj", [P, 2, NPAIR, NB], F32, GR + 29056)
    last = at("last", [P, 2, 9, NPAIR], F32, GR + 31104)
    sm = [at(f"sm{i}", [P, NPAIR], F32, GR + 31104 + 128 * i) for i in range(15)]
    via_ = at("via", [P, NPAIR], F32, WK + 50368)
    smi = at("smi", [P, NPAIR], I32, GR + 31104 + 128 * 17)
    mask = at("mask", [P, 384], F32, GR + 33408)
    reset = at("reset", [P, T], F32, GR + 34944)
    rdec = at("rdec", [P, NPAIR], F32, GR + 36096)
    params = at("params", [P, 96], F32, GR + 36224)
    wtok = at("wtok", [P, 2, IH], F32, GR + 36608)
    parity = at("parity", [P, 4], F32, GR + 36800)
    half = at("half", [P, 2], F32, GR + 36832)
    nramp = at("nramp", [P, 32], F32, GR + 36672)
    kidx = at("kidx", [P, NB * NPAGES, DI], F32, WK)
    kidxd = at("kidxd", [P, 4, 2, DI], F32, WK + 22528)
    kis = at("kis", [P, NB, SK], F32, WK + 4096)
    qiT = at("qiT", [P, 4, T], F32, WK + 12416)
    kiT = at("kiT", [P, T], F32, WK + 17024)
    wiT = at("wiT", [IH, T], F32, WK + 18176)
    qibd = at("qibd", [P, NB, 32], F32, WK + 19328)
    rels = at("rels", [P, 2, SK], F32, WK + 20352)
    rel = [at(f"rel{i}", [P, 1024], F32, (WK, QT + 4608)[i]) for i in range(2)]
    e16 = at("e16", [P, 16], F32, GR + 33024)
    m3 = at("m3", [P, 8, 16], F32, KT + 3584)
    wz = at("wz", [P, 2, 32], F32, 7008)
    wcol = at("wcol", [P, 2], F32, GR + 33088)
    keep = at("keep", [TS, DS], F32, GR + 33120)
    nkeep = at("nkeep", [TS, DS], F32, GR + 33152)
    sc = [at("sc0", [P, 128], F32, WK + 45056), at("sc1", [P, 256], F32, WK + 45568), at("scs", [TS, SK], F32, WK + 46592)]
    wk = [at("wk0", [P, 128], F32, WK + 47648), at("wk1", [P, 256], F32, WK + 48160), at("wks", [TS, SK], F32, WK + 49184)]
    top8 = [at(f"top8_{i}", [P, 8], F32, WK + 50240 + 32 * i) for i in range(4)]
    gt = [at(f"gt{i}", [P, 2, T], F32, WK + 2304 * i) for i in range(2)]
    t1 = at("t1", [P, 2, T], F32, WK + 4608)
    t2 = at("t2", [P, 2, T], F32, WK + 6912)
    ws = [at(f"ws{i}", [P, 2, T], F32, WK + 9216 + 2304 * i) for i in range(2)]
    xs = [at(f"xs{i}", [P, 2, T], F32, WK + 13824 + 2304 * i) for i in range(4)]
    xb = at("xb", [P, 2, T], F32, WK + 23040)
    tab = [at(f"tab{i}", [P, 2, T], F32, WK + 25344 + 2304 * i) for i in range(2)]
    tqs = [at(f"tq{i}", [P, 2, 16, 16], F32, WK + (29952, 40064)[i]) for i in range(2)]
    rm = [at(f"rm{i}", [P, T], F32, WK + 32256 + 1152 * i) for i in range(2)]
    lbs = at("lbs", [P, 2, P], F32, WK + 34560)
    cbs = at("cbs", [P, 2, P], F32, WK + 35584)
    us = at("us", [P, T], F32, WK + 36608)
    ys = at("ys", [P, T], F32, WK + 37760)
    zs = at("zs", [P, T], F32, WK + 38912)
    lastt = at("lastt", [P, 2, 3, P], F32, WK + 40064)
    att_hi = at("att_hi", [P, 8, T], F32R, RE)
    att_lo = at("att_lo", [P, 8, T], F32R, RE + 9216)
    yb = at("yb", [P, KD, T], F32, RE + 18432)
    gbt = at("gbt", [P, 2, T], F32, WK + 4608)
    glu_gate = at("glu_gate", [P, 2, T], F32, WK + 9216)
    qs = at("qs", [P, T], F32, WK + 11520)
    ks = at("ks", [P, T], F32, WK + 12672)
    vs = at("vs", [P, 2, P], F32, WK + 40064)
    kTb = at("kTb", [P, NPR, SK], F32, WK + 41088)
    qbs = at("qbs", [P, NPR, 32], F32, WK + 43168)
    psb = at("psb", [64, SK], F32, WK + 16160)
    pTb = at("pTb", [P, 3, 64], F32, WK + 17216)
    smax = at("smax", [64, 8], F32, WK + 18016)
    glu_a = at("glu_a", [P, 2, T], F32, WK + 19456)
    ps = at("ps", [P, 2, 384], F32, WK + 25344)
    pTs = at("pTs", [P, 2, 384], F32, WK + 28416)
    pmax = at("pmax", [P, 3, 2, 2], F32, WK + 31488)
    kpg = [at(f"kpg{i}", [P, NPAGES, KV], F32, GR + 2048 * i) for i in range(2)]
    vpg = [at(f"vpg{i}", [P, NPAGES, KV], F32, GR + 4096 + 2048 * i) for i in range(2)]
    vnew = [at(f"vnew{i}", [DS, KV], F32, GR + 8192 + 1024 * i) for i in range(2)]
    spare = at("spare", [P, 8], F32, WK + 43424)
    maskb = [at(f"maskb{i}", [64, SK], F32, GR + 10240 + 1056 * i) for i in range(2)]
    ga = at("ga", [P, KD, T], F32, GR + 12416)
    mg = [at(f"mg{i}", [P, 2, T], F32, WK + 23424 + 2304 * i) for i in range(2)]
    m_hi = at("m_hi", [P, KD, T], F32R, UZ)
    m_lo = at("m_lo", [P, KD, T], F32R, UZ + 18432)
    x2 = at("x2", [P, KD, T], F32, UZ + 36864)
    sq2 = at("sq2", [P, 2, T], F32, WK + 28032)
    h2_hi = at("h2_hi", [P, KD, T], F32R, GR)
    h2_lo = at("h2_lo", [P, KD, T], F32R, GR + 18432)
    LU = 2 + TP + NB * (2 + DS)
    a_hi = at("a_hi", [P, KF, T], F32R, RE)
    a_lo = at("a_lo", [P, KF, T], F32R, RE + 50688)
    up = at("up", [P, 4, LU], F32, WK + 32512)
    mix = at("mix", [P, 4, LU], F32, WK + 37408)
    cstate = at("cstate", [P, 2 * KF, 18], F32, WK + 42304)
    cnat_in = at("cnat_in", [P, 11, P], F32, WK + 32512)
    cnat_out = at("cnat_out", [P, 13, P], F32, WK + 32512)
    sq3 = at("sq3", [P, 2, T], F32, WK + 39168)
    x3 = at("x3", [P, KD, T], F32, GR)
    xg = at("xg", [P, KD, T], F32, GR + 18432)
    yo = at("yo", [P, 3, D], F32, RE)

    banks = nc.alloc_psum_tensor("banks", [P, 8, 512], F32)
    acc = banks[:, 0:4, :]
    aux = banks[:, 4:8, :]

    with ExitStack() as ctx:
        signals = {}

        def sem(name):
            if name not in signals:
                signals[name] = ctx.enter_context(nc.semaphore(name))
            return signals[name]

        hi_ready, lo_ready, chunks_used = sem("hi_ready"), sem("lo_ready"), sem("chunks_used")
        raw_in = [sem(f"raw_in{i}") for i in range(NSLOT)]
        acc_free = [sem(f"acc_free{i}") for i in range(2)]

        def loop(engine, start, end):
            return nc.Fori(start, end, engines=(ENGINES[engine],), hint_back_edge=True)

        def by_kv(t, s):
            return t[:, s, :, :].rearrange("p t (n g d) -> p t n g d", n=2, g=2)

        def by_query(t, s):
            return t[:, s, :, :].rearrange("p t (g n d) -> p t g n d", n=2, g=2)

        def sample_half(n):
            return aux[DH * n:DH * (n + 1), 3, TP:TP + 64].rearrange("p (a n g t) -> p a n g t", a=2, n=2, g=4)[:, :, n, :, :]

        def sample_cols(tile, rows, b):
            return tile[rows, :, ds(TP + DS * b, DS)].rearrange("p (a g) t -> p a g t", a=2)

        w_proj = I["w_attn_proj"].rearrange("(k g d) n -> k d g n", k=NKV, g=GQ)

        def sample_new(tile, it, m):
            return tile[:, ds(2 * it + m, 1), TP:T].rearrange("p o (b t) -> p (o b) t", b=NB)

        def sample_mix(m):
            return mix[:, 2 + m, 2 + TP:LU].rearrange("p (b t) -> p b t", b=NB)[:, :, 0:DS]

        def new_states(h):
            return up[:, 2 * h:2 * h + 2, TP - 4:LU].rearrange("p a (k s) -> p a k s", s=6)[:, :, :, 4:6]

        w_rows = {n: W_.rearrange("(t p) n -> p t n", p=P) for n, W_ in I.items() if n in (
            "w_in", "w_glu", "w_out", "w_up", "w_down")}

        block = ctx.enter_context(nc.Block())

        @block.sync
        def _(sp):
            for b in range(2):
                sp.dma_start(xin[:, b, :], I["x_prompt"][b * P:(b + 1) * P, :]).then_inc(sem(f"x_in{b}"), 16)
            sp.dma_start(xin[0:TS, 2, :], I["x_sample"]).then_inc(sem("x_in2"), 16)

            def slot_free(c, first=False):
                if not first:
                    sp.wait_ge(lo_ready, c - 3)

            def load(w, c, q, kt, col, first=False):
                slot_free(c + q, first)
                for h in range(2):
                    sp.dma_start(raw[:, q % NSLOT, 2 * h:2 * h + 2, :], w_rows[w][:, kt + 2 * h:kt + 2 * h + 2, ds(col, CW)]
                                 ).then_inc(raw_in[q % NSLOT], 16)

            def group(w, c, nk, col, first=False, at=0):
                for q in range(nk // KCH):
                    load(w, c - at, at + q, KCH * q, col, first)

            for k in range(4):
                group("w_in", C_U + 4 * k, KD, CU + CW * k, first=k == 0)
            for q in range(4):
                slot_free(C_KIWI + q)
                rows = w_rows["w_in"][:, KCH * q:KCH * q + KCH, :]
                sp.dma_start(raw[:, q, :, DI:2 * DI + IH], rows[:, :, CKI:CKI + DI + IH]).then_inc(raw_in[q], 16)
                sp.dma_start(raw[:, q, :, 0:DI], rows[:, :, CKI:CKI + DI]).then_inc(raw_in[q], 16)
            for k in range(2):
                group("w_in", C_QI + 4 * k, KD, CQI + CW * k)
            group("w_in", C_KV, KD, CK)
            group("w_in", C_KV + 4, KD, CV)
            for j in range(NPR):
                for gp in range(2):
                    for q in range(4):
                        slot_free(C_Q + 8 * j + 4 * gp + q)
                        for n in range(2):
                            col = (2 * j + n) * KV + gp * P
                            sp.dma_start(raw[:, q, :, P * n:P * (n + 1)], w_rows["w_in"][:, KCH * q:KCH * q + KCH, col:col + P]
                                         ).then_inc(raw_in[q], 16)
            with loop("SP", 0, N_GATE) as it:
                group("w_in", C_GATE + 8 * it, KD, CGA + 2 * CW * it)
                group("w_in", C_GATE + 8 * it + 4, KD, CGA + CW + 2 * CW * it)
            sp.wait_ge(sem("vs_stored"), 16)
            with loop("SP", 0, 4) as turn:
                for u in range(2):
                    i = 2 * turn + u
                    group("w_glu", C_GLU + 4 * i, 8, D + CW * i)
                    pages = [sp.value_load(ptab[0:1, ds(NPAGES * i + g, 1)], min_val=0, max_val=NPOOL - 1) for g in range(NPAGES)]
                    sp.wait_ge(sem("unit_free"), i + 1)
                    sp.dma_start(vnew[u][:, :], O["v_sample"][ds(DS * i, DS), :]).then_inc(sem(f"v_in{u}"), 16)
                    for g, page in enumerate(pages):
                        sp.dma_start(kpg[u][:, g:g + 1, :], I["cache_k"][ds(page, 1)].rearrange("a p d -> p a d")).then_inc(sem(f"k_in{u}"), 16)
                        sp.dma_start(vpg[u][:, g:g + 1, :], I["cache_v"][ds(page, 1)].rearrange("a p d -> p a d")).then_inc(sem(f"v_in{u}"), 16)
                    group("w_glu", C_GLU + 4 * i + 2, 8, CW * (i + 1) - CW, at=2)
                    sp.wait_ge(sem("mask_out"), 16)
                    sp.dma_start(maskb[u][:, :], bc(W["mask"][ds(DS * i, DS), :], 0, 16)).then_inc(sem(f"mask_in{u}"), 16)
            with loop("SP", 0, N_PROJ) as it:
                for s in range(2):
                    for q in range(2):
                        slot = 2 * s + q
                        slot_free(C_PROJ + 4 * it + slot)
                        for n in range(2):
                            sp.dma_start(raw[DH * n:DH * (n + 1), slot, :, :], w_proj[2 * q + n][:, :, ds(2 * CW * it + CW * s, CW)]
                                         ).then_inc(raw_in[slot], 16)
            with loop("SP", 0, N_OUT) as it:
                for s in range(2):
                    group("w_out", C_OUT + 8 * it + 4 * s, KD, 2 * CW * it + CW * s)
            with loop("SP", 0, N_UP) as it:
                for s in range(2):
                    group("w_up", C_UP + 8 * it + 4 * s, KD, FF * s + CW * it)
            with loop("SP", 0, 2) as half:
                for g in range(4):
                    for q in range(KF // KCH):
                        k = KF // KCH * g + q
                        load("w_down", C_END + 44 * half + k - k % 4, k % 4, KCH * q, 4 * CW * half + CW * g)

        @block.tensor
        def _(pe):
            def group(g_parity, use, c, nk, xh, xl, widths=(P, P), before={}, slot0=0):
                if not (isinstance(use, int) and use == 0):
                    pe.wait_ge(acc_free[g_parity], use)
                for q in range(nk // KCH):
                    for step in before.get(q, ()):
                        step()
                    pe.wait_ge(lo_ready, c + q + 1)
                    for k in range(KCH):
                        kt = KCH * q + k
                        for m, w in enumerate(widths):
                            out = acc[0:w, 2 * g_parity + m, 0:T]
                            h = whi[:, (slot0 + q) % NSLOT, k, m * P:m * P + w]
                            lo = wlo[:, (slot0 + q) % NSLOT, k, m * P:m * P + w]
                            pe.matmul(out, h, xh[:, kt, :], start=kt == 0, stop=False)
                            pe.matmul(out, h, xl[:, kt, :], start=False, stop=False)
                            mm = pe.matmul(out, lo, xh[:, kt, :], start=False, stop=kt == nk - 1)
                    mm.then_inc(chunks_used, 1)

            def transpose(out, in_):
                k = in_.shape[0]
                b = in_.base_partition() if callable(in_.base_partition) else in_.base_partition
                return pe.matmul(out, in_, ident[b:b + k, b:b + k], is_transpose=True)

            pe.wait_ge(sem("consts_ready"), 1)
            pe.wait_ge(sem("nv_in"), 64)
            transpose(aux[:, 3, 0:56], nvn[:, :]).then_inc(sem("nv_t"), 1)
            for b in range(3):
                pe.wait_ge(sem(f"x_in{b}"), 16)
            for kt in range(KD):
                if kt >= 3:
                    pe.wait_ge(sem("hhi_ready"), kt - 2)
                    pe.wait_ge(sem("xt_done"), kt - 2)
                for b, n in ((0, P), (1, P), (2, TS)):
                    last_t = transpose(aux[:, kt % 3, b * P:b * P + n], xin[0:n, b, kt * P:(kt + 1) * P])
                last_t.then_inc(sem("xt_ready"), 1)
            group(0, 0, C_U, KD, hhi, hlo)
            pe.wait_ge(sem("nv_ready"), 1)
            pe.wait_ge(sem("cv_in"), 64)
            for j in range(4):
                t = transpose(aux[:, 3, j * 88:(j + 1) * 88], cvn[:, j, :])
            t.then_inc(sem("par_t"), 1)
            pe.wait_ge(sem("par_ready"), 1)
            pe.wait_ge(sem("ap_in"), 32)
            pe.wait_ge(sem("lstep_wide"), 1)
            transpose(aux[:, 3, 0:96], apn[:, :]).then_inc(sem("par_t"), 1)
            pe.wait_ge(sem("par_ready"), 2)
            pe.wait_ge(sem("st_in"), 32)
            for c in range(2):
                for h in range(2):
                    t = transpose(aux[:, 3, (2 * c + h) * P:(2 * c + h + 1) * P], stn[:, c, h, :])
            t.then_inc(sem("par_t"), 1)
            pe.wait_ge(sem("diag_ready"), 3)
            pe.wait_ge(sem("par_ready"), 3)
            for b, n in ((0, P), (1, P), (2, TS)):
                mm = pe.matmul(aux[:, 3, b * P:b * P + n], ones[0:n, :], sqx[0:n, b * P:b * P + n], start=True, stop=True)
            mm.then_inc(sem("rb_ready"), 1)
            group(1, 0, C_U + 4, KD, hhi, hlo)
            group(0, 1, C_U + 8, KD, hhi, hlo)
            group(1, 1, C_U + 12, KD, hhi, hlo)
            group(0, 2, C_KIWI, KD, hhi, hlo, widths=(P, IH))
            group(1, 2, C_QI, KD, hhi, hlo)
            group(0, 3, C_QI + 4, KD, hhi, hlo)
            group(1, 3, C_KV, KD, hhi, hlo)
            group(0, 4, C_KV + 4, KD, hhi, hlo)

            for r in range(4):
                pe.wait_ge(sem("kidx_dup"), r + 1)
                pe.wait_ge(sem("rstd_ready"), 1)
                for k in range(4):
                    t = transpose(aux[:, r, k * P:(k + 1) * P], kidxd[:, k, :, :].rearrange("p a d -> p (a d)"))
                t.then_inc(sem("kit_t"), 1)
            pe.wait_ge(acc_free[1], 4)
            pe.wait_ge(acc_free[0], 5)
            for b, n in ((0, P), (1, P), (2, TS)):
                pe.wait_ge(sem("kit_ready"), b + 1)
                for j in range(NPR):
                    transpose(aux[0:n, b, j * P:(j + 1) * P], kT[:, j, b * P:b * P + n])
                    t = transpose(aux[0:n, b, KV + j * P:KV + (j + 1) * P], vT[:, j, b * P:b * P + n])
                t.then_inc(sem("tok_t"), 1)
            pe.wait_ge(sem("kit_ready"), 4)
            for b, n in ((0, P), (1, P), (2, TS)):
                transpose(aux[0:n, 3, b * DI:(b + 1) * DI], kiT[0:DI, b * P:b * P + n])
            for b in range(2):
                t = transpose(aux[:, 3, 192 + b * IH:192 + (b + 1) * IH], wiT[:, b * P:(b + 1) * P])
            t.then_inc(sem("tok_t"), 1)

            def q_pair(j):
                group(1, 4 + j, C_Q + 8 * j, KD, hhi, hlo)
                group(0, 5 + j, C_Q + 8 * j + 4, KD, hhi, hlo)

            def index_scores(bank, b, heads, keys):
                for h in heads:
                    r0, k = DI * (h % 2), (h - heads[0]) // 2 * keys
                    mm = pe.matmul(aux[:, bank + h % 2, k:k + keys], qiT[r0:r0 + DI, h // 2, b * P:(b + 1) * P],
                                   kiT[r0:r0 + DI, 0:keys], start=True, stop=True)
                mm.then_inc(sem("isc_t"), 1)

            q_pair(0)
            pe.wait_ge(sem("tok_ready"), 2)
            index_scores(0, 0, range(8), P)
            pe.wait_ge(sem("tok_ready"), 5)
            index_scores(2, 1, range(4), TP)
            pe.wait_ge(sem("isc_relu"), 1)
            index_scores(0, 1, range(4, 8), TP)
            pe.wait_ge(sem("isc_relu"), 2)
            pe.wait_ge(sem("qibd_ready"), 2)
            for b in range(NB):
                mm = pe.matmul(aux[32 * (b % 4):32 * (b % 4) + 32, 2 + b // 4, 0:SK], qibd[:, b, :], kis[:, b, :], start=True, stop=True)
            mm.then_inc(sem("isc_t"), 1)
            q_pair(1)
            pe.wait_ge(sem("isc_relu"), 4)
            pe.wait_ge(sem("wz_ready"), 2)
            for h in range(2):
                mm = pe.matmul(aux[0:TS, 0, 0:SK], wz[:, h, :], rels[:, h, :], start=h == 0, stop=h == 1)
            mm.then_inc(sem("ssc_t"), 1)
            pe.wait_ge(sem("bc_ready"), 1)
            pe.wait_ge(sem("scs_ready"), 1)
            for r in range(8):
                src = bdg[:, r // 2, :, :].rearrange("p (j i) c -> p j (i c)", i=4) if r < 4 else cdg[:, (r - 4) // 2, :, :]
                if r >= 3:
                    pe.wait_ge(sem("bct_ready"), r - 2)
                for k in range(4):
                    t = transpose(aux[:, r % 3, k * P:(k + 1) * P], src[:, 4 * (r % 2) + k, :])
                t.then_inc(sem("bct_t"), 1)
            def s5_inputs(it, i):
                pe.wait_ge(sem("s5_staged"), it + 1)
                if not (isinstance(it, int) and i == 0):
                    pe.wait_ge(sem("bu_used"), 4 * it + i)
                r = slice(32 * i, 32 * i + 32)
                for c in range(2):
                    mm = pe.matmul(aux[:, c, 0:T], lbs[r, c, :], us[r, :], start=True, stop=True)
                mm.then_inc(sem("bu_ready"), 1)

            def s5_outputs(jt):
                pe.wait_ge(sem("cbs_staged"), jt + 1)
                pe.wait_ge(sem("xs_ready"), 8 * jt + 8)
                for i in range(4):
                    r = slice(32 * i, 32 * i + 32)
                    for c in range(2):
                        mm = pe.matmul(aux[r, 2, 0:T], cbs[:, c, r], xs[i][:, c, :], start=c == 0, stop=c == 1)
                mm.then_inc(sem("y_ready"), 1)

            def gates(it, first=False):
                c = C_GATE + 8 * it
                ahead = () if first else (lambda: s5_outputs(it - 1),)
                group(1, 6 + it, c, KD, hhi, hlo, before={0: (lambda: s5_inputs(it, 0),), 2: ahead + (lambda: s5_inputs(it, 1),)})
                group(0, 7 + it, c + 4, KD, hhi, hlo, before={0: (lambda: s5_inputs(it, 2),), 2: (lambda: s5_inputs(it, 3),)})

            pe.wait_ge(sem("bct_ready"), 8)
            gates(0, first=True)
            with loop("PE", 1, N_GATE) as it:
                gates(it)
            def prompt_scores(i):
                pe.wait_ge(sem("unit_staged"), 3 * i + 3)
                for n in range(2):
                    r = slice(DH * n, DH * (n + 1))
                    for b in range(2):
                        mm = pe.matmul(aux[:, n, P * b:P * b + P * (b + 1)], qs[r, P * b:P * (b + 1)], ks[r, 0:P * (b + 1)], start=True, stop=True)
                mm.then_inc(sem("s_ready"), 1)

            def cached_keys(i, u, turn):
                pe.wait_ge(sem(f"k_in{u}"), 32 * turn + 32)
                pe.wait_ge(lo_ready, C_GLU + 4 * i + 2)
                for p in range(NPR):
                    for g in range(NPAGES):
                        t = transpose(aux[:, 2, (2 * p + g) * P:(2 * p + g + 1) * P], kpg[u][:, g, P * p:P * (p + 1)])
                t.then_inc(sem("kt_t"), 1)

            def sample_scores(i):
                pe.wait_ge(sem("kTb_ready"), i + 1)
                pe.wait_ge(sem("new_ready"), 3 * i + 3)
                pe.wait_ge(acc_free[0], 15 + i)
                for p in range(NPR):
                    mm = pe.matmul(aux[32 * p:32 * p + 32, 3, 0:SK], qbs[:, p, :], kTb[:, p, :], start=True, stop=True)
                mm.then_inc(sem("ss_t"), 1)

            def prompt_probs(i):
                pe.wait_ge(sem("p_ready"), i + 1)
                for n in range(2):
                    for m in range(3):
                        t = transpose(aux[:, n, m * P:(m + 1) * P], ps[:, n, m * P:(m + 1) * P])
                t.then_inc(sem("pt_t"), 1)

            def sample_probs(i):
                for m, n in ((0, P), (1, P), (2, DS)):
                    t = transpose(aux[0:n, 3, 64 * m:64 * (m + 1)], psb[:, m * P:m * P + n])
                t.then_inc(sem("spt_t"), 1)

            def prompt_values(i):
                pe.wait_ge(sem("sp_ready"), i + 1)
                pe.wait_ge(sem("pT_ready"), i + 1)
                for n in range(2):
                    o = aux[:, 2, TP * n:TP * (n + 1)]
                    pe.matmul(o[:, 0:P], vs[:, 0, :], pTs[:, n, 0:P], start=True, stop=True)
                    pe.matmul(o[:, P:TP], vs[:, 0, :], pTs[:, n, P:TP], start=True, stop=False)
                    mm = pe.matmul(o[:, P:TP], vs[:, 1, :], pTs[:, n, TP:384], start=False, stop=True)
                mm.then_inc(sem("o_ready"), 1)

            def sample_values(i, u, turn):
                pe.wait_ge(sem("pTb_ready"), i + 1)
                pe.wait_ge(sem(f"v_in{u}"), 48 * turn + 48)
                for p in range(NPR):
                    o = aux[:, 3, TP + 32 * p:TP + 32 * (p + 1)]
                    c = slice(P * p, P * (p + 1))
                    for g in range(NPAGES):
                        pe.matmul(o, vpg[u][:, g, c], pTb[:, g, 32 * p:32 * (p + 1)], start=g == 0, stop=False)
                    mm = pe.matmul(o, vnew[u][:, c], pTb[0:DS, 2, 32 * p:32 * (p + 1)], start=False, stop=True)
                mm.then_inc(sem("unit_free"), 1)


            def unit(i, u, turn, first=False):
                c = C_GLU + 4 * i
                start = (lambda: prompt_scores(i), lambda: cached_keys(i, u, turn))
                middle = (lambda: sample_scores(i),)
                if first:
                    middle = (lambda: s5_outputs(N_GATE - 1), start[0], lambda: pe.wait_ge(sem("ys_ready"), N_GATE), start[1],
                              lambda: pe.wait_ge(sem("z_ready"), NUT), middle[0])
                    start = ()
                group(1, 14 + i, c, 8, zhi, zlo, before={0: start, 1: middle})
                group(0, 15 + i, c + 2, 8, zhi, zlo, slot0=2, before={0: (lambda: prompt_probs(i),),
                                                                      1: (lambda: prompt_values(i), lambda: sample_probs(i))})
                sample_values(i, u, turn)

            pe.wait_ge(sem("z_ready"), NUT - 1)
            unit(0, 0, 0, first=True)
            unit(1, 1, 0)
            with loop("PE", 1, 4) as turn:
                for u in range(2):
                    unit(2 * turn + u, u, turn)
            pe.wait_ge(sem("last_ready"), 2 * NPAIR)
            for c in range(2):
                rows = last[:, c, :, :].rearrange("p k i -> p (k i)")
                for m, n in ((0, P), (1, P), (2, NPAIR)):
                    t = transpose(aux[0:n, c, m * P:(m + 1) * P], rows[:, m * P:m * P + n])
            t.then_inc(sem("last_t"), 1)
            pe.wait_ge(sem("att_done"), 8)
            pe.wait_ge(sem("atts_done"), 8)
            with loop("PE", 0, N_PROJ) as it:
                group(1, 22 + it, C_PROJ + 4 * it, 8, att_hi, att_lo)
                group(0, 23 + it, C_PROJ + 4 * it + 2, 8, att_hi, att_lo, slot0=2)
            pe.wait_ge(sem("cn_in2"), 16 * 8)
            pe.wait_ge(sem("last_copied"), 2)
            for r in range(11):
                t = transpose(aux[:, r // 4, (r % 4) * P:(r % 4 + 1) * P], cnat_in[:, r, :])
            t.then_inc(sem("cst_t"), 1)
            pe.wait_ge(sem("m_ready"), 6)
            group(1, 26, C_OUT, KD, m_hi, m_lo, before={3: (lambda: pe.wait_ge(sem("m_ready"), 8),)})
            group(0, 27, C_OUT + 4, KD, m_hi, m_lo)
            with loop("PE", 1, N_OUT) as it:
                group(1, 26 + it, C_OUT + 8 * it, KD, m_hi, m_lo)
                group(0, 27 + it, C_OUT + 8 * it + 4, KD, m_hi, m_lo)
            def token_sums():
                pe.wait_ge(sem("sq_done"), 8)
                pe.matmul(aux[:, 3, 0:T], ones[:, :], sqacc[:, :], start=True, stop=True).then_inc(sem("sum_ready"), 1)

            pe.wait_ge(sem("h2_ready"), 6)
            group(1, 30, C_UP, KD, h2_hi, h2_lo, before={1: (token_sums,), 3: (lambda: pe.wait_ge(sem("h2_ready"), 8),)})
            group(0, 31, C_UP + 4, KD, h2_hi, h2_lo)
            with loop("PE", 1, N_UP) as it:
                group(1, 30 + it, C_UP + 8 * it, KD, h2_hi, h2_lo)
                group(0, 31 + it, C_UP + 8 * it + 4, KD, h2_hi, h2_lo)
            pe.wait_ge(sem("cst_saved"), 2 * N_UP + 1)
            for r in range(13):
                n = min(126, 18 * (2 * KF - 7 * r))
                t = transpose(aux[0:n, r // 4, (r % 4) * P:(r % 4 + 1) * P], cstate[:, 7 * r:7 * r + n // 18, :].rearrange("p a b -> p (a b)"))
            t.then_inc(sem("cst_t"), 1)
            with loop("PE", 0, 2) as half:
                for g in range(4):
                    group((g + 1) % 2, 52 + 2 * half + (g + 1) // 2, C_END + 44 * half + 11 * g, KF, a_hi, a_lo, slot0=11 * g % 4,
                          before={10: (lambda: pe.wait_ge(sem("a_ready"), N_UP),)})
            pe.wait_ge(sem("xg_ready"), 8)
            for b, n in ((0, P), (1, P), (2, TS)):
                for k in range(4):
                    t = 4 * b + k
                    if t == 3:
                        pe.wait_ge(sem("sq_done"), 16)
                        for b_, n_ in ((0, P), (1, P), (2, TS)):
                            mm = pe.matmul(aux[0:n_, 3, b_:b_ + 1], sqacc[:, b_ * P:b_ * P + n_], ones[:, 0:1], start=True, stop=True)
                        mm.then_inc(sem("sum_ready"), 1)
                    if t >= 3:
                        pe.wait_ge(sem("yo_ready"), t - 2)
                    for m in range(4):
                        mm = transpose(aux[0:n, t % 3, m * P:(m + 1) * P], xg[:, 4 * k + m, b * P:b * P + n])
                    mm.then_inc(sem("yo_t"), 1)

        @block.scalar
        def _(act):
            own = Own(act, sem("act_own"))

            def hi(c, q, cols=CW, first=False):
                s = q % NSLOT
                act.wait_ge(raw_in[s], 32 * ((c + q - s) // 4 + 1) if isinstance(c, int) else 32 * (c // 4 + q // 4 + 1))
                if not first:
                    act.wait_ge(chunks_used, c + q - 3)
                act.activation(whi[:, s, :, 0:cols], raw[:, s, :, 0:cols], ACT.Copy).then_inc(hi_ready, 1)

            def hi_q(c, q):
                act.wait_ge(raw_in[q], 32 * (c // 4 + 1))
                act.wait_ge(chunks_used, c + q - 3)
                for g in range(2):
                    ins = act.activation(by_query(whi, q)[:, :, g, :, :], by_kv(raw, q)[:, :, :, g, :], ACT.Copy)
                ins.then_inc(hi_ready, 1)

            for k, (n, rows) in enumerate((("norm_mix", 16), ("norm_ffn", 16), ("norm_final", 16), ("s5_d", 8))):
                act.dma_start(nvn[16 * k:16 * k + rows, :], I[n].rearrange("(t p) -> t p", p=P)).then_inc(sem("nv_in"), 16)
            act.wait_ge(sem("nv_t"), 1)
            act.activation(nvec[:, :], aux[:, 3, 0:56], ACT.Copy).then_inc(sem("nv_ready"), 1)
            act.wait_ge(sem("nv_ready"), 1)
            for kt in range(KD):
                act.wait_ge(sem("xt_ready"), kt + 1)
                act.activation(hhi[:, kt, :], aux[:, kt % 3, 0:T], ACT.Copy, scale=nvec[:, kt:kt + 1]).then_inc(sem("hhi_ready"), 1)
                if kt % 4 == 3:
                    hi(C_U, kt // 4, first=True)
            act.wait_ge(sem("xt_done"), KD)
            act.dma_start(W["x_kept"], xt0[:, :, :].rearrange("p k t -> p (k t)")).then_inc(sem("x_kept"), 16)
            act.wait_ge(sem("consts_ready"), 2)
            for b, n in ((0, P), (1, P), (2, TS)):
                if b:
                    act.wait_ge(sem("ss_ready"), b)
                act.activation(sqx[0:n, :], xin[0:n, b, :], ACT.Square, accum_out=rtok[0:n, b:b + 1]).then_inc(sem("ss_ready"), 1)
            act.wait_ge(sem("par_t"), 1)
            act.activation(convp[:, :, :].rearrange("p a b -> p (a b)"), aux[:, 3, 0:352], ACT.Copy).then_inc(sem("par_ready"), 1)
            act.wait_ge(sem("par_t"), 2)
            act.activation(params[:, :], aux[:, 3, 0:96], ACT.Copy).then_inc(sem("par_ready"), 1)
            act.wait_ge(sem("par_t"), 3)
            act.activation(x0[:, :, :, :].rearrange("p c b i -> p (c b i)"), aux[:, 3, :], ACT.Copy).then_inc(sem("par_ready"), 1)
            act.wait_ge(sem("ms_ready"), 1)
            act.activation(rtok[:, 4:7], rtok[:, 0:3], ACT.Sqrt).then_inc(sem("root_ready"), 1)

            for g in range(1, 4):
                for q in range(4):
                    hi(C_U + 4 * g, q)
            for q in range(4):
                hi(C_KIWI, q, cols=2 * DI + IH)
            for g in range(2):
                act.activation(tqs[0][:, g, 0:4, :], ident[:, :].rearrange("p (a g c) -> p a g c", a=4, g=2)[:, :, g, :], ACT.Copy,
                               accum_out=parity[:, g:g + 1]).then_inc(sem("parity_sum"), 1)
            act.wait_ge(sem("parity_sum"), 2)
            act.activation(parity[:, 2:4], parity[:, 0:2], ACT.Copy, scale=-1.0).then_inc(sem("parity_ready"), 1)
            for c in (C_QI, C_QI + 4, C_KV, C_KV + 4):
                for q in range(4):
                    hi(c, q)
            for q in range(4):
                hi_q(C_Q, q)
            for r in range(4):
                act.wait_ge(sem("kit_t"), r + 1)
                act.activation(kis[:, 2 * r:2 * r + 2, 0:PAST], aux[:, r, :].rearrange("p (b s) -> p b s", b=2), ACT.Copy).then_inc(sem("kit_ready"), 1)
            for b, n in ((0, P), (1, P), (2, TS)):
                act.wait_ge(sem("tok_t"), b + 1)
                act.activation(ktok[0:n, b, :], aux[0:n, b, 0:KV], ACT.Copy).then_inc(sem("ktok_ready"), 1)
                act.activation(vtok[:, b, :] if b < 2 else vstok[:, :], aux[0:n, b, KV:2 * KV], ACT.Copy).then_inc(sem("tok_ready"), 1)
            act.wait_ge(sem("tok_t"), 4)
            act.activation(kitok[:, 0:2, :], aux[:, 3, 0:2 * DI].rearrange("p (b d) -> p b d", b=2), ACT.Copy).then_inc(sem("ktok_ready"), 1)
            act.activation(kitok[0:TS, 2, :], aux[0:TS, 3, 2 * DI:3 * DI], ACT.Copy).then_inc(sem("tok_ready"), 1)
            act.activation(wtok[:, :, :], aux[:, 3, 192:192 + 2 * IH].rearrange("p (b h) -> p b h", b=2), ACT.Copy,
                           scale=DI ** -0.5 * IH ** -0.5).then_inc(sem("tok_ready"), 1)
            act.wait_ge(sem("tok_ready"), 5)
            act.wait_ge(sem("ktok_ready"), 4)
            for b in range(2):
                act.dma_start(O["k_prompt"][b * P:(b + 1) * P, :], ktok[:, b, :]).then_inc(sem("tok_stored"), 16)
                act.dma_start(O["v_prompt"][b * P:(b + 1) * P, :], vtok[:, b, :]).then_inc(sem("tok_stored"), 16)
                act.dma_start(O["kidx_prompt"][b * P:(b + 1) * P, :], kitok[:, b, :]).then_inc(sem("tok_stored"), 16)
            act.dma_start(O["k_sample"], ktok[0:TS, 2, :]).then_inc(sem("tok_stored"), 16)
            act.dma_start(O["kidx_sample"], kitok[0:TS, 2, :]).then_inc(sem("tok_stored"), 16)
            act.dma_start(O["v_sample"], vstok[:, :]).then_inc(sem("vs_stored"), 16)
            for b in range(NB):
                act.dma_start(W["wi"][b % 4, :, :, b // 4], wiT[:, TP + DS * b:TP + DS * (b + 1)], allow_slow_non_contiguous=True
                              ).then_inc(sem("wi_out"), 16)
            for q in range(4):
                hi_q(C_Q + 4, q)
            act.wait_ge(sem("angles_ready"), 1)
            own.link(act.activation(tmp[2][:, :, :], tmp[2][:, :, :], ACT.Sin))
            own.link(act.activation(tmp[3][:, :, :], tmp[3][:, :, :], ACT.Sin))
            for i, (dst, src, s) in enumerate(((e2[:, 0:NPAIR, 0, :], tmp[3][:, :, 0:16], 1.0), (e2[:, 0:NPAIR, 1, :], tmp[2][:, :, 0:16], 1.0),
                                               (e1[:, 0:NPAIR, 0, :], tmp[3][:, :, 16:32], 1.0), (e1[:, 0:NPAIR, 1, :], tmp[2][:, :, 16:32], 1.0),
                                               (e1r[:, 0:NPAIR, 0, :], tmp[2][:, :, 16:32], -1.0), (e1r[:, 0:NPAIR, 1, :], tmp[3][:, :, 16:32], 1.0))):
                act.activation(dst, src, ACT.Copy, scale=s).then_inc(sem("sines_ready"), 1)
            act.wait_ge(sem("wi_out"), 16 * NB)
            act.dma_start(wcol[:, :], W["wi"].rearrange("b h t f -> (b h t) f")).then_inc(sem("wcol_in"), 16)

            for q in range(4):
                hi_q(C_Q + 8, q)
            act.wait_ge(sem("isc_t"), 1)
            act.activation(rel[0][:, :], aux[:, 0:2, :].rearrange("p a c -> p (a c)"), ACT.Relu).then_inc(sem("isc_relu"), 1)
            act.wait_ge(sem("isc_t"), 2)
            act.activation(rel[1][:, :], aux[:, 2:4, :].rearrange("p a c -> p (a c)"), ACT.Relu).then_inc(sem("isc_relu"), 1)
            act.wait_ge(sem("isc_t"), 3)
            act.wait_ge(sem("isc_sum"), 1)
            act.activation(rel[0][:, :], aux[:, 0:2, :].rearrange("p a c -> p (a c)"), ACT.Relu).then_inc(sem("isc_relu"), 1)
            act.wait_ge(sem("isc_t"), 4)
            act.activation(rels[:, :, :], aux[:, 2:4, 0:SK], ACT.Relu).then_inc(sem("isc_relu"), 1)
            for q in range(4):
                hi_q(C_Q + 12, q)
            for r in range(8):
                act.wait_ge(sem("bct_t"), r + 1)
                dst = (lbt if r < 4 else cbt)[:, (r // 2) % 2, 4 * (r % 2):4 * (r % 2) + 4, :]
                act.activation(dst.rearrange("p j c -> p (j c)"), aux[:, r % 3, :], ACT.Copy).then_inc(sem("bct_ready"), 1)
            def stage_s5(it, first=False):
                if not first:
                    act.wait_ge(sem("bu_ready"), 4 * it)
                ins = act.activation(us[:, :], uT[:, ds(it, 1), :].rearrange("p o t -> p (o t)"), ACT.Copy)
                if first:
                    ins.then_inc(sem("gates_out0"), 16)
                act.activation(lbs[:, :, :], lbt[:, :, ds(it, 1), :].rearrange("p c o m -> p c (o m)"), ACT.Copy).then_inc(sem("s5_staged"), 1)

            def decay_row(it, i, first=False):
                if not (first and i < 2):
                    act.wait_ge(sem("ws_ready"), 4 * it + i - 1)
                act.activation(rm[i % 2][:, :], reset[:, :], ACT.Copy, scale=rdec[:, ds(4 * it + i, 1)]).then_inc(sem("rm_ready"), 1)

            def store_gates(par, n, tile):
                act.wait_ge(acc_free[par], n)
                act.activation(gt[par][:, :, :], gt[par][:, :, :], ACT.Sigmoid).then_inc(sem("gate_done"), 1)
                act.wait_ge(sem("gate_done"), 2 * n - 14 + par)
                act.dma_start(W["gates"][ds(tile, 2)].rearrange("a p t -> p a t"), gt[par][:, :, :]).then_inc(sem(f"gates_out{par}"), 16)

            def gelu(jt):
                act.wait_ge(sem("ys_ready"), jt + 1)
                act.activation(zs[:, :], ys[:, :], ACT.Gelu_apprx_tanh).then_inc(sem("zs_ready"), 1)
                act.wait_ge(sem("zs_ready"), jt + 1)
                act.activation(zhi[:, ds(jt, 1), :].rearrange("p o t -> p (o t)"), zs[:, :], ACT.Copy).then_inc(sem("zhi_ready"), 1)

            def gates(it, first=False):
                c = C_GATE + 8 * it
                hi(c, 0)
                hi(c, 1)
                stage_s5(it, first)
                decay_row(it, 0, first)
                decay_row(it, 1, first)
                hi(c, 2)
                if not first:
                    store_gates(0, 7 + it, 4 * it - 2)
                hi(c, 3)
                decay_row(it, 2)
                hi(c, 4)
                if not first:
                    gelu(it - 1)
                if not first:
                    act.wait_ge(sem("y_ready"), it)
                act.activation(cbs[:, :, :], cbt[:, :, ds(it, 1), :].rearrange("p c o m -> p c (o m)"), ACT.Copy).then_inc(sem("cbs_staged"), 1)
                hi(c, 5)
                decay_row(it, 3)
                hi(c, 6)
                hi(c, 7)
                store_gates(1, 7 + it, 4 * it)

            gates(0, first=True)
            with loop("Activation", 1, N_GATE) as it:
                gates(it)
            for k in range(2):
                act.activation(spare[:, k:k + 1], ident[:, 0:1], ACT.Copy).then_inc(sem("unit_free"), 1)
            hi(C_GLU, 0)
            hi(C_GLU, 1)
            store_gates(0, 7 + N_GATE, 4 * N_GATE - 2)
            gelu(N_GATE - 1)
            with loop("Activation", 0, 4) as turn:
                own.loop(turn, 2)
                for u in range(2):
                    i = 2 * turn + u
                    c = C_GLU + 4 * i
                    act.wait_ge(sem("kt_t"), i + 1)
                    act.activation(kTb[:, :, 0:PAST], aux[:, 2, :].rearrange("p (a s) -> p a s", a=NPR), ACT.Copy).then_inc(sem("kTb_ready"), 1)
                    hi(c, 2)
                    act.wait_ge(sem("max_ready"), i + 1)
                    for b in range(2):
                        for n in range(2):
                            keys = ps[:, n, P * b:P * b + P * (b + 1)]
                            ins = act.activation(keys, keys, ACT.Exp, bias=pmax[:, 0, b, n:n + 1], accum_out=pmax[:, 1, b, n:n + 1])
                    ins.then_inc(sem("exp_ready"), 1)
                    hi(c, 3)
                    act.wait_ge(sem("smax_ready"), i + 1)
                    act.activation(psb[:, :], psb[:, :], ACT.Exp, bias=smax[:, 0:1], accum_out=smax[:, 1:2]).then_inc(sem("sexp_ready"), 1)
                    act.wait_ge(sem("pt_t"), i + 1)
                    act.activation(pTs[:, :, :], aux[:, 0:2, 0:384], ACT.Copy).then_inc(sem("pT_ready"), 1)
                    act.wait_ge(acc_free[0], 15 + i)
                    act.activation(glu_gate[:, :, :], acc[:, 2:4, 0:T], ACT.Sigmoid).then_inc(acc_free[1], 1)
                    hi(c, 4)
                    act.wait_ge(sem("spt_t"), i + 1)
                    own(act.activation(pTb[:, 0:2, :], aux[:, 3, 0:P].rearrange("p (a s) -> p a s", a=2), ACT.Copy))
                    act.activation(pTb[0:DS, 2, :], aux[0:DS, 3, P:P + 64], ACT.Copy).then_inc(sem("pTb_ready"), 1)
                    act.wait_ge(sem("o_ready"), i + 1)
                    for n in range(2):
                        r = slice(DH * n, DH * (n + 1))
                        ins = act.activation(att_hi[r, ds(i, 1), 0:TP].rearrange("p o t -> p (o t)"), aux[r, 2, TP * n:TP * (n + 1)], ACT.Copy)
                    ins.then_inc(sem("att_hi_ready"), 1)
                    hi(c, 5)
                    act.wait_ge(sem("unit_free"), i + 3)
                    for n in range(2):
                        r = slice(DH * n, DH * (n + 1))
                        ins = act.activation(sample_cols(att_hi, r, i), sample_half(n), ACT.Copy)
                    ins.then_inc(sem("atts_hi_ready"), 1)
            own.done(4)
            for t in range(8):
                act.dma_start(cnat_in[16 * t:16 * t + 16, :, :], I["state_ffn_conv"].rearrange("b s (r t p) -> t (b s) r p", t=8, p=P)[t]
                              ).then_inc(sem("cn_in2"), 16)
            act.wait_ge(sem("glu_free"), 9)
            act.wait_ge(sem("atts_done"), 8)
            act.dma_start(x2[:, :, :].rearrange("p k t -> p (k t)"), W["x_kept"]).then_inc(sem("x2_in"), 16)
            act.wait_ge(sem("last_t"), 1)
            act.activation(lastt[:, :, 0:2, :], aux[:, 0:2, 0:2 * P].rearrange("p c (m q) -> p c m q", m=2), ACT.Copy).then_inc(sem("last_copied"), 1)
            act.activation(lastt[0:NPAIR, :, 2, :], aux[0:NPAIR, 0:2, 2 * P:3 * P], ACT.Copy).then_inc(sem("last_copied"), 1)
            act.wait_ge(sem("last_copied"), 2)
            for c in range(2):
                rows = O["s5_state"][c].rearrange("k i p -> (k i) p")
                act.dma_start(rows[0:2 * P, :].rearrange("(m q) p -> q m p", m=2), lastt[:, c, 0:2, :]).then_inc(sem("s5_stored"), 16)
                act.dma_start(rows[2 * P:9 * NPAIR, :], lastt[0:NPAIR, c, 2, :]).then_inc(sem("s5_stored"), 16)

            def round_merged(g, s):
                act.wait_ge(sem("mg_ready"), g + 1)
                act.activation(m_hi[:, ds(2 * g, 2), :], mg[s][:, :, :], ACT.Copy).then_inc(sem("m_hi_ready"), 1)

            with loop("Activation", 0, N_PROJ) as it:
                for s in range(2):
                    hi(C_PROJ + 4 * it, 2 * s + 2)
                    hi(C_PROJ + 4 * it, 2 * s + 3)
                    round_merged(2 * it + s, s)
            hi(C_OUT, 2)
            hi(C_OUT, 3)
            act.wait_ge(sem("s5_stored"), 64)
            act.wait_ge(sem("cst_t"), 1)
            for r in range(3):
                n = 8 * min(4, 11 - 4 * r)
                act.activation(cstate[:, 32 * r:32 * r + n, 0:16], aux[:, r, 0:16 * n].rearrange("p (a b) -> p a b", b=16), ACT.Copy
                               ).then_inc(sem("cst_ready"), 1)
            with loop("Activation", 0, N_OUT) as it:
                for s in range(2):
                    g = 2 * it + s
                    for q in range(4 * s + 4, 4 * s + 8):
                        hi(C_OUT + 8 * it, q)
                    act.wait_ge(acc_free[1 - s], 27 + it + s)
                    for m in range(2):
                        ins = act.activation(h2_hi[:, ds(2 * g + m, 1), :].rearrange("p o t -> p (o t)"),
                                             x2[:, ds(2 * g + m, 1), :].rearrange("p o t -> p (o t)"), ACT.Copy, scale=nvec[:, ds(16 + 2 * g + m, 1)])
                    ins.then_inc(sem("h2_hi_ready"), 1)
            act.dma_start(W["x_kept"], x2[:, :, :].rearrange("p k t -> p (k t)")).then_inc(sem("x2_kept"), 16)
            act.wait_ge(sem("ms_ready"), 2)
            act.activation(nw[1][:, :], nw[0][:, :], ACT.Sqrt).then_inc(sem("root_ready"), 1)
            with loop("Activation", 0, N_UP) as it:
                c = C_UP + 8 * it
                for q in range(4, 8):
                    hi(c, q)
                act.wait_ge(sem("conv_done"), 2 * it + 1)
                act.activation(mix[:, 0:2, 0:LU - 2], mix[:, 0:2, 0:LU - 2], ACT.Silu).then_inc(sem("silu_ready"), 1)
                for q in range(8, 12):
                    hi(c, q)
                act.wait_ge(sem("x2_kept"), 16)
                act.wait_ge(sem("prod_ready"), it + 1)
                act.activation(a_hi[:, ds(2 * it, 2), 0:TP], mix[:, 2:4, 0:TP], ACT.Copy)
                act.activation(sample_new(a_hi, it, 0), sample_mix(0), ACT.Copy)
                act.activation(sample_new(a_hi, it, 1), sample_mix(1), ACT.Copy).then_inc(sem("a_hi_ready"), 1)
            act.wait_ge(chunks_used, C_END)
            act.wait_ge(sem("x2_kept"), 16)
            act.dma_start(x3[:, :, :].rearrange("p k t -> p (k t)"), W["x_kept"]).then_inc(sem("x3_in"), 16)
            act.wait_ge(sem("cst_t"), 2)
            act.wait_ge(sem("a_ready"), N_UP)
            for r in range(4):
                w = P * min(4, 13 - 4 * r)
                n = 126 if r < 3 else 72
                act.activation(cnat_out[0:n, 4 * r:4 * r + w // P, :], aux[0:n, r, 0:w].rearrange("p (a b) -> p a b", b=P), ACT.Copy
                               ).then_inc(sem("crow_ready"), 1)
            for half in range(2):
                for g in range(4):
                    c = C_END + 44 * half + 11 * g
                    for q in range(4, 15):
                        if c + q < C_END + 88:
                            hi(c - c % 4, q + c % 4)
                    k = 4 * half + g
                    act.wait_ge(acc_free[(g + 1) % 2], 53 + k // 2 + k % 2)
                    for m in range(2):
                        ins = act.activation(xg[:, 2 * k + m, :], x3[:, 2 * k + m, :], ACT.Copy, scale=nvec[:, 32 + 2 * k + m:33 + 2 * k + m])
                    ins.then_inc(sem("xg_ready"), 1)
            act.wait_ge(sem("ms_ready"), 3)
            act.activation(rtok[:, 4:7], rtok[:, 0:3], ACT.Sqrt).then_inc(sem("root_ready"), 1)
            act.wait_ge(sem("rtok_ready"), 1)
            for b, n in ((0, P), (1, P), (2, TS)):
                for k in range(4):
                    act.wait_ge(sem("yo_t"), 4 * b + k + 1)
                    act.activation(yo[0:n, b, 4 * P * k:4 * P * (k + 1)], aux[0:n, (4 * b + k) % 3, :], ACT.Copy, scale=rtok[0:n, 4 + b:5 + b]
                                   ).then_inc(sem("yo_ready"), 1)
                act.wait_ge(sem("yo_ready"), 4 * b + 4)
                act.dma_start(O["y_prompt"][b * P:b * P + n, :] if b < 2 else O["y_sample"], yo[0:n, b, :]).then_inc(sem("y_stored"), 16)
            act.wait_ge(sem("y_stored"), 48)
            act.wait_ge(sem("tok_stored"), 16 * 8)
            act.wait_ge(sem("s5_stored"), 64)
            act.wait_ge(sem("crow_stored"), 16 * 11)

        @block.vector
        def _(dve):
            own = Own(dve, sem("dve_own"))

            def lo(c, q, cols=CW):
                s = q % NSLOT
                dve.wait_ge(hi_ready, c + q + 1)
                dve.tensor_tensor(wlo[:, s, :, 0:cols], raw[:, s, :, 0:cols], whi[:, s, :, 0:cols], ALU.subtract).then_inc(lo_ready, 1)

            def lo_q(c, q):
                dve.wait_ge(hi_ready, c + q + 1)
                for g in range(2):
                    ins = dve.tensor_tensor(by_query(wlo, q)[:, :, g, :, :], by_kv(raw, q)[:, :, :, g, :],
                                            by_query(whi, q)[:, :, g, :, :], ALU.subtract)
                ins.then_inc(lo_ready, 1)

            def evac(dst, parity, c_end):
                dve.wait_ge(chunks_used, c_end)
                dve.tensor_tensor(dst, acc[:, 2 * parity:2 * parity + 2, 0:T], bc(rstd[:, :], 1, 2), ALU.mult).then_inc(acc_free[parity], 1)

            dve.wait_ge(sem("nv_ready"), 1)
            for kt in range(KD):
                dve.wait_ge(sem("hhi_ready"), kt + 1)
                dve.tensor_copy(xt0[:, kt, :], aux[:, kt % 3, 0:T])
                dve.scalar_tensor_tensor(hlo[:, kt, :], aux[:, kt % 3, 0:T], nvec[:, kt:kt + 1], hhi[:, kt, :],
                                         ALU.mult, ALU.subtract).then_inc(sem("xt_done"), 1)
                if kt % 4 == 3:
                    lo(C_U, kt // 4)

            def inverse_root(v, y, t, root_done):
                root_done()
                own.link(dve.reciprocal(y, y))
                own.link(dve.tensor_tensor(t, y, y, ALU.mult))
                own.link(dve.tensor_tensor(t, t, v, ALU.mult))
                own.link(dve.tensor_scalar(t, t, -0.5, 1.5, ALU.mult, ALU.add))

            dve.wait_ge(sem("ss_ready"), 3)
            dve.tensor_scalar(rtok[:, 0:3], rtok[:, 0:3], 1.0 / D, EPS, ALU.mult, ALU.add).then_inc(sem("ms_ready"), 1)
            inverse_root(rtok[:, 0:3], rtok[:, 4:7], sqx[:, 600:603], lambda: dve.wait_ge(sem("root_ready"), 1))
            own.link(dve.tensor_tensor(rtok[:, 4:7], rtok[:, 4:7], sqx[:, 600:603], ALU.mult))
            for b, n in ((0, P), (1, P), (2, TS)):
                dve.tensor_scalar(sqx[0:n, b * P:b * P + n], ident[0:n, 0:n], rtok[0:n, 4 + b:5 + b], None, ALU.mult
                                  ).then_inc(sem("diag_ready"), 1)
            for q in range(4):
                lo(C_U + 4, q)
            dve.wait_ge(sem("den_sum"), 1)
            dve.reciprocal(sm[8][:, :], sm[8][:, :]).then_inc(sem("den_ready"), 1)
            dve.wait_ge(sem("rb_ready"), 1)
            dve.tensor_copy(rstd[:, :], aux[:, 3, 0:T]).then_inc(sem("rstd_ready"), 1)
            dve.wait_ge(sem("rstd_ready"), 1)
            dve.wait_ge(sem("x_kept"), 16)
            evac(uT[:, 0:2, :], 0, C_U + 4)
            dve.wait_ge(sem("m3_ready"), 1)
            own(dve.memset(wz[:, :, :], 0.0))
            own(dve.tensor_reduce(e16[:, :], m3[:, :, :].rearrange("p h c -> p c h"), AX_X, ALU.add))
            own.link(dve.tensor_reduce(keep[:, :], ident[0:TS, 0:TS].rearrange("p (b t) -> p t b", b=NB), AX_X, ALU.add))
            for t in (2, 1, 0):
                own.link(dve.tensor_tensor(keep[:, t:t + 1], keep[:, t:t + 1], keep[:, t + 1:t + 2], ALU.add))
            own(dve.tensor_scalar(nkeep[:, :], keep[:, :], -1.0, -NEG, ALU.add, ALU.mult))
            for k in range(1, 4):
                for q in range(4):
                    lo(C_U + 4 * k + 4, q, cols=CW if k < 3 else 2 * DI + IH)
                evac(uT[:, 2 * k:2 * k + 2, :], k % 2, C_U + 4 * k + 4)
            for q in range(4):
                lo(C_QI, q)
            dve.wait_ge(chunks_used, C_KIWI + 4)
            dve.tensor_tensor(kiT[:, :], acc[:, 0, 0:T], rstd[:, :], ALU.mult)
            dve.tensor_tensor(wiT[:, :], acc[0:IH, 1, 0:T], rstd[0:IH, :], ALU.mult).then_inc(acc_free[0], 1)
            for k, (dst, par) in enumerate(((qiT[:, 0:2, :], 1), (qiT[:, 2:4, :], 0), (kT[:, :, :], 1))):
                for q in range(4):
                    lo(C_QI + 4 * k + 4, q)
                evac(dst, par, C_QI + 4 * k + 4)
            for q in range(4):
                lo_q(C_Q, q)
            evac(vT[:, :, :], 0, C_KV + 8)
            dve.wait_ge(sem("kidx_in"), 16 * NB * NPAGES)
            for r in range(4):
                if r:
                    dve.wait_ge(sem("kit_t"), r)
                dve.tensor_copy(kidxd[:, :, :, :], bc(kidx[:, 4 * r:4 * r + 4, :], 2, 2)).then_inc(sem("kidx_dup"), 1)
            for q in range(4):
                lo_q(C_Q + 4, q)
            evac(qT[:, 0:2, :], 1, C_Q + 4)
            dve.wait_ge(sem("kit_ready"), 4)
            dve.tensor_copy(kis[:, :, PAST:SK], kiT[:, TP:T].rearrange("p (b t) -> p b t", b=NB))
            own.link(dve.memset(qibd[:, :, :], 0.0))
            for h in range(2):
                dve.tensor_copy(qibd[DI * h:DI * (h + 1), :, :].rearrange("p b (c h t) -> p b c h t", c=4, h=2)[:, :, :, h, :],
                                qiT[DI * h:DI * (h + 1), :, TP:T].rearrange("p c (b t) -> p b c t", b=NB)).then_inc(sem("qibd_ready"), 1)
            dve.wait_ge(sem("wcol_in"), 16)
            for h in range(2):
                dve.tensor_scalar(wz[:, h, 16 * h:16 * h + 16], e16[:, :], wcol[:, h:h + 1], DI ** -0.5 * IH ** -0.5, ALU.mult, ALU.mult
                                  ).then_inc(sem("wz_ready"), 1)
            for q in range(4):
                lo_q(C_Q + 8, q)
            evac(qT[:, 2:4, :], 0, C_Q + 8)

            def head_sum(out, src, keys, b, h0, n, signal=None):
                for h in range(n):
                    w = wtok[:, b, h0 + h:h0 + h + 1]
                    k = (h % 2 * n // 2 + h // 2) * keys
                    if h0 + h == 0:
                        ins = dve.tensor_scalar(out, src[:, k:k + keys], w, None, ALU.mult)
                    else:
                        ins = dve.scalar_tensor_tensor(out, src[:, k:k + keys], w, out, ALU.mult, ALU.add)
                    if signal and h == n - 1:
                        ins.then_inc(sem(signal), 1)
                    else:
                        own.link(ins)

            dve.wait_ge(sem("tok_ready"), 5)
            dve.wait_ge(sem("cdg_ready"), 1)
            dve.wait_ge(sem("isc_relu"), 1)
            head_sum(sc[0][:, :], rel[0], P, 0, 0, 8, "isc_sum")
            dve.wait_ge(sem("isc_relu"), 2)
            head_sum(sc[1][:, :], rel[1], TP, 1, 0, 4)
            dve.wait_ge(sem("isc_relu"), 3)
            head_sum(sc[1][:, :], rel[0], TP, 1, 4, 4, "isc_sum")
            for q in range(4):
                lo_q(C_Q + 12, q)
            evac(qT[:, 4:6, :], 1, C_Q + 12)
            dve.wait_ge(sem("ssc_t"), 1)
            dve.tensor_copy(sc[2][:, 0:PAST], aux[0:TS, 0, 0:PAST])
            own.link(dve.tensor_tensor(sc[2][:, PAST:SK], aux[0:TS, 0, PAST:SK], keep[:, :], ALU.mult))
            dve.tensor_tensor(sc[2][:, PAST:SK], sc[2][:, PAST:SK], nkeep[:, :], ALU.add).then_inc(sem("scs_ready"), 1)
            def pair(it, i, c, q, first=False):
                dve.wait_ge(sem("tab_ready"), 12 * it + 3 * i + 3)
                grid = tab[i % 2][:, :, 0:TP].rearrange("p c (a b) -> p c a b", a=16)
                own(dve.tensor_tensor(grid, tqs[i % 2][:, :, :, :], grid, ALU.add))
                lo(c, q)
                own.wait()
                dve.wait_ge(sem("bu_ready"), 4 * it + i + 1)
                if not (first and i == 0):
                    dve.wait_ge(sem("ws_ready"), 4 * it + i)
                own(dve.tensor_tensor(t1[:, :, :], aux[:, 0:2, 0:T], bc(tab[i % 2][:, 0, :], 1, 2), ALU.mult))
                dve.tensor_tensor(t2[:, :, :], aux[:, 0:2, 0:T], bc(tab[i % 2][:, 1, :], 1, 2), ALU.mult).then_inc(sem("bu_used"), 1)
                lo(c, q + 1)
                dve.wait_ge(sem("bu_used"), 4 * it + i + 1)
                own(dve.tensor_tensor(t1[:, 0, :], t1[:, 0, :], t2[:, 1, :], ALU.add))
                own.link(dve.tensor_tensor(t1[:, 1, :], t1[:, 1, :], t2[:, 0, :], ALU.subtract))
                first_in = t1[:, :, TP:T].rearrange("p c (b t) -> p c b t", b=NB)[:, :, :, 0]
                own.link(dve.tensor_tensor(first_in, first_in, inj[:, :, ds(4 * it + i, 1), :].rearrange("p c o b -> p c (o b)"), ALU.add))
                dve.wait_ge(sem("rm_ready"), 4 * it + i + 1)
                if not (first and i < 2):
                    dve.wait_ge(sem("xs_ready"), 8 * it + 2 * i - 2)
                for c in range(2):
                    ins = dve.tensor_tensor_scan(ws[i % 2][:, c, :], rm[i % 2][:, :], t1[:, c, :], 0.0, ALU.mult, ALU.add)
                ins.then_inc(sem("ws_ready"), 1)

            def top_max(first):
                for k in range(3):
                    n = P if k < 2 else TS
                    own(dve.max(top8[k][0:n, :], (sc[k] if first else wk[k])[:, :]))

            def top_out(first):
                for k in range(3):
                    n = P if k < 2 else TS
                    own(dve.match_replace(wk[k][:, :], top8[k][0:n, :], (sc[k] if first else wk[k])[:, :], NEG))

            def skip(jt):
                dve.wait_ge(sem("y_ready"), jt + 1)
                dve.scalar_tensor_tensor(ys[:, :], uT[:, ds(jt, 1), :].rearrange("p o t -> p (o t)"), nvec[:, ds(48 + jt, 1)],
                                         aux[:, 2, 0:T], ALU.mult, ALU.add).then_inc(sem("ys_ready"), 1)

            def z_low(jt):
                dve.wait_ge(sem("zhi_ready"), jt + 1)
                dve.tensor_tensor(zlo[:, ds(jt, 1), :].rearrange("p o t -> p (o t)"), zs[:, :],
                                  zhi[:, ds(jt, 1), :].rearrange("p o t -> p (o t)"), ALU.subtract).then_inc(sem("z_ready"), 1)

            def gate_evac(par, n, c_end, first=False):
                if not first:
                    dve.wait_ge(sem(f"gates_out{par}"), 16 * (n - 6))
                evac(gt[par][:, :, :], par, c_end)

            def gates(it, first=False):
                c = C_GATE + 8 * it
                pair(it, 0, c, 0, first)
                if first:
                    evac(qT[:, 6:8, :], 0, c)
                else:
                    gate_evac(0, 6 + it, c)
                pair(it, 1, c, 2, first)
                if not first:
                    skip(it - 1)
                pair(it, 2, c, 4, first)
                gate_evac(1, 6 + it, c + 4, first)
                top_max(first)
                if not first:
                    z_low(it - 1)
                pair(it, 3, c, 6, first)
                top_out(first)

            dve.wait_ge(sem("sc_masked"), 2)
            dve.wait_ge(sem("scs_ready"), 1)
            dve.wait_ge(sem("tok_stored"), 16 * 8)
            dve.wait_ge(sem("vs_stored"), 16)
            gates(0, first=True)
            with loop("DVE", 1, N_GATE) as it:
                own.loop(it - 1, 26)
                gates(it)
            own.done(N_GATE - 1)
            lo(C_GLU, 0)
            lo(C_GLU, 1)
            gate_evac(0, 6 + N_GATE, C_GLU)
            skip(N_GATE - 1)
            own.link(dve.memset(top8[3][0:TS, :], NEG))
            own.link(dve.max(top8[2][0:TS, :], wk[2][:, :]))
            own.link(dve.tensor_copy(top8[3][0:TS, 0:1], top8[2][0:TS, 0:1]))
            own.link(dve.match_replace(wk[2][:, :], top8[3][0:TS, :], wk[2][:, :], NEG))
            out_of = (mask[:, 0:P], mask[:, P:3 * P], wk[2][:, :])
            for k in range(3):
                own(dve.tensor_tensor(out_of[k], wk[k][:, :], sc[k][:, :], ALU.is_equal))
            own.wait()
            for k in range(3):
                ins = dve.tensor_scalar(out_of[k], out_of[k], -1.0e30, None, ALU.mult)
            ins.then_inc(sem("masks_ready"), 1)
            z_low(N_GATE - 1)
            dve.wait_ge(sem("masks_ready"), 1)
            with loop("DVE", 0, 4) as turn:
                own.loop(turn, 16)
                for u in range(2):
                    i = 2 * turn + u
                    c = C_GLU + 4 * i
                    dve.wait_ge(sem("s_ready"), i + 1)
                    own.link(dve.scalar_tensor_tensor(ps[:, :, :], aux[:, 0:2, 0:384], DH ** -0.5, bc(mask[:, :], 1, 2), ALU.mult, ALU.add))
                    own(dve.tensor_reduce(pmax[:, 0, 0, :], ps[:, :, 0:P], AX_X, ALU.max))
                    own.link(dve.tensor_reduce(pmax[:, 0, 1, :], ps[:, :, P:3 * P], AX_X, ALU.max))
                    dve.tensor_scalar(pmax[:, 0, :, :], pmax[:, 0, :, :], -1.0, None, ALU.mult).then_inc(sem("max_ready"), 1)
                    lo(c, 2)
                    dve.wait_ge(sem("exp_ready"), i + 1)
                    own.link(dve.reciprocal(pmax[:, 2, :, :], pmax[:, 1, :, :]))
                    own(dve.tensor_tensor(ps[:, :, 0:P], ps[:, :, 0:P], bc(pmax[:, 2, 0, :], 2, P), ALU.mult))
                    dve.tensor_tensor(ps[:, :, P:3 * P], ps[:, :, P:3 * P], bc(pmax[:, 2, 1, :], 2, TP), ALU.mult).then_inc(sem("p_ready"), 1)
                    dve.wait_ge(sem("ss_t"), i + 1)
                    dve.wait_ge(sem(f"mask_in{u}"), 16 * turn + 16)
                    own.link(dve.scalar_tensor_tensor(psb[:, :], aux[0:64, 3, 0:SK], DH ** -0.5, maskb[u][:, :], ALU.mult, ALU.add))
                    own.link(dve.tensor_reduce(smax[:, 0:1], psb[:, :], AX_X, ALU.max))
                    dve.tensor_scalar(smax[:, 0:1], smax[:, 0:1], -1.0, None, ALU.mult).then_inc(sem("smax_ready"), 1)
                    lo(c, 3)
                    dve.wait_ge(sem("sexp_ready"), i + 1)
                    own.link(dve.reciprocal(smax[:, 2:3], smax[:, 1:2]))
                    dve.tensor_scalar(psb[:, :], psb[:, :], smax[:, 2:3], None, ALU.mult).then_inc(sem("sp_ready"), 1)
                    lo(c, 4)
                    dve.wait_ge(sem("att_hi_ready"), i + 1)
                    for n in range(2):
                        r = slice(DH * n, DH * (n + 1))
                        ins = dve.tensor_tensor(att_lo[r, ds(i, 1), 0:TP].rearrange("p o t -> p (o t)"), aux[r, 2, TP * n:TP * (n + 1)],
                                                att_hi[r, ds(i, 1), 0:TP].rearrange("p o t -> p (o t)"), ALU.subtract)
                    ins.then_inc(sem("att_done"), 1)
                    lo(c, 5)
                    dve.wait_ge(sem("atts_hi_ready"), i + 1)
                    for n in range(2):
                        r = slice(DH * n, DH * (n + 1))
                        ins = dve.tensor_tensor(sample_cols(att_lo, r, i), sample_half(n), sample_cols(att_hi, r, i), ALU.subtract)
                    ins.then_inc(sem("atts_done"), 1)
                    dve.wait_ge(chunks_used, c + 4)
                    dve.wait_ge(acc_free[1], 15 + i)
                    dve.wait_ge(sem("glu_free"), i + 1)
                    dve.tensor_tensor(glu_a[:, :, :], acc[:, 0:2, 0:T], glu_gate[:, :, :], ALU.mult).then_inc(acc_free[0], 1)
            own.done(4)
            dve.wait_ge(sem("ga_in"), 16)
            with loop("DVE", 0, N_PROJ) as it:
                for s in range(2):
                    g = 2 * it + s
                    lo(C_PROJ + 4 * it, 2 * s + 2)
                    lo(C_PROJ + 4 * it, 2 * s + 3)
                    dve.wait_ge(chunks_used, C_PROJ + 4 * it + 2 * s + 2)
                    dve.wait_ge(lo_ready, C_PROJ + 4 * it + 2 * s + 4)
                    dve.tensor_tensor(mg[s][:, :, :], acc[:, 2 - 2 * s:4 - 2 * s, 0:T], ga[:, ds(2 * g, 2), :], ALU.mult).then_inc(acc_free[1 - s], 1)
                    dve.wait_ge(acc_free[1 - s], 23 + it + s)
                    dve.tensor_tensor(mg[s][:, :, :], mg[s][:, :, :], yb[:, ds(2 * g, 2), :], ALU.add).then_inc(sem("mg_ready"), 1)
                    dve.wait_ge(sem("m_hi_ready"), g + 1)
                    dve.wait_ge(sem("mg_ready"), g + 1)
                    dve.tensor_tensor(m_lo[:, ds(2 * g, 2), :], mg[s][:, :, :], m_hi[:, ds(2 * g, 2), :], ALU.subtract).then_inc(sem("m_ready"), 1)
            lo(C_OUT, 2)
            dve.wait_ge(sem("x2_in"), 16)
            with loop("DVE", 0, N_OUT) as it:
                for s in range(2):
                    g = 2 * it + s
                    for q in range(4 * s + 3, 4 * s + 7):
                        lo(C_OUT + 8 * it, q)
                    dve.wait_ge(chunks_used, C_OUT + 8 * it + 4 * s + 4)
                    dve.tensor_tensor(x2[:, ds(2 * g, 2), :], acc[:, 2 - 2 * s:4 - 2 * s, 0:T], x2[:, ds(2 * g, 2), :], ALU.add).then_inc(acc_free[1 - s], 1)
                    dve.wait_ge(sem("h2_hi_ready"), g + 1)
                    for m in range(2):
                        tile = lambda a: a[:, ds(2 * g + m, 1), :].rearrange("p o t -> p (o t)")
                        ins = dve.scalar_tensor_tensor(tile(h2_lo), tile(x2), nvec[:, ds(16 + 2 * g + m, 1)], tile(h2_hi), ALU.mult, ALU.subtract)
                    ins.then_inc(sem("h2_ready"), 1)
            dve.wait_ge(sem("sum_ready"), 1)
            dve.tensor_scalar(nw[0][:, :], aux[:, 3, 0:T], 1.0 / D, EPS, ALU.mult, ALU.add).then_inc(sem("ms_ready"), 1)
            inverse_root(nw[0][:, :], nw[1][:, :], rstd[:, :], lambda: dve.wait_ge(sem("root_ready"), 2))
            own.link(dve.tensor_tensor(rstd[:, :], nw[1][:, :], rstd[:, :], ALU.mult))

            def up_evac(it, s):
                dve.wait_ge(chunks_used, C_UP + 8 * it + 4 * s + 4)
                dve.wait_ge(sem("cst_saved"), 2 * it + 1)
                dve.wait_ge(lo_ready, C_UP + 8 * it + 4 * s + 7)
                m = slice(2 * s, 2 * s + 2)
                a = acc[:, 2 - 2 * s:4 - 2 * s, :]
                own(dve.tensor_tensor(up[:, m, 2:2 + TP], a[:, :, 0:TP], bc(rstd[:, 0:TP], 1, 2), ALU.mult))
                for k in range(2):
                    new = up[:, 2 * s + k, 2 + TP:LU].rearrange("p (b t) -> p b t", b=NB)[:, :, 2:2 + DS]
                    ins = dve.tensor_tensor(new, a[:, k, TP:T].rearrange("p (b t) -> p b t", b=NB),
                                            rstd[:, TP:T].rearrange("p (b t) -> p b t", b=NB), ALU.mult)
                ins.then_inc(acc_free[1 - s], 1)

            def conv(it, s):
                dve.wait_ge(acc_free[1 - s], 31 + it + s)
                dve.wait_ge(sem("cst_in_up"), it + 1)
                for m in range(2):
                    t = KF * s + m + 2 * it
                    own(dve.tensor_scalar(mix[:, 2 * s + m, 0:LU - 2], up[:, 2 * s + m, 0:LU - 2], convp[:, 0, ds(t, 1)], convp[:, 3, ds(t, 1)], ALU.mult, ALU.add))
                for j in (1, 2):
                    own.wait()
                    for m in range(2):
                        t = KF * s + m + 2 * it
                        ins = dve.scalar_tensor_tensor(mix[:, 2 * s + m, 0:LU - 2], up[:, 2 * s + m, j:j + LU - 2], convp[:, j, ds(t, 1)], mix[:, 2 * s + m, 0:LU - 2],
                                                       ALU.mult, ALU.add)
                        if j == 2 and m == 1:
                            ins.then_inc(sem("conv_done"), 1)
                        else:
                            own(ins)

            with loop("DVE", 0, N_UP) as it:
                own.loop(it, 14)
                c = C_UP + 8 * it
                for q in range(3, 7):
                    lo(c, q)
                up_evac(it, 0)
                conv(it, 0)
                for q in range(7, 11):
                    lo(c, q)
                up_evac(it, 1)
                conv(it, 1)
                dve.wait_ge(sem("silu_ready"), it + 1)
                dve.wait_ge(sem("conv_done"), 2 * it + 2)
                dve.tensor_tensor(mix[:, 2:4, 0:LU - 2], mix[:, 0:2, 0:LU - 2], mix[:, 2:4, 0:LU - 2], ALU.mult).then_inc(sem("prod_ready"), 1)
                dve.wait_ge(sem("a_hi_ready"), it + 1)
                dve.wait_ge(sem("prod_ready"), it + 1)
                own(dve.tensor_tensor(a_lo[:, ds(2 * it, 2), 0:TP], mix[:, 2:4, 0:TP], a_hi[:, ds(2 * it, 2), 0:TP], ALU.subtract))
                own(dve.tensor_tensor(sample_new(a_lo, it, 0), sample_mix(0), sample_new(a_hi, it, 0), ALU.subtract))
                dve.tensor_tensor(sample_new(a_lo, it, 1), sample_mix(1), sample_new(a_hi, it, 1), ALU.subtract).then_inc(sem("a_ready"), 1)
            own.done(N_UP)
            for half in range(2):
                for g in range(4):
                    c = C_END + 44 * half + 11 * g
                    for q in range(3, 14):
                        if c + q < C_END + 88:
                            lo(c - c % 4, q + c % 4)
                    k = 4 * half + g
                    par = (g + 1) % 2
                    if k == 0:
                        dve.wait_ge(sem("x3_in"), 16)
                    dve.wait_ge(chunks_used, c + 11)
                    dve.tensor_tensor(x3[:, 2 * k:2 * k + 2, :], acc[:, 2 * par:2 * par + 2, 0:T], x3[:, 2 * k:2 * k + 2, :], ALU.add
                                      ).then_inc(acc_free[par], 1)
            dve.wait_ge(sem("sum_ready"), 2)
            own(dve.memset(rtok[:, 0:3], 1.0))
            own.wait()
            own.link(dve.tensor_scalar(rtok[:, 0:2], aux[:, 3, 0:2], 1.0 / D, EPS, ALU.mult, ALU.add))
            dve.tensor_scalar(rtok[0:TS, 2:3], aux[0:TS, 3, 2:3], 1.0 / D, EPS, ALU.mult, ALU.add).then_inc(sem("ms_ready"), 1)
            inverse_root(rtok[:, 0:3], rtok[:, 4:7], nw[0][:, 0:3], lambda: dve.wait_ge(sem("root_ready"), 3))
            dve.tensor_tensor(rtok[:, 4:7], rtok[:, 4:7], nw[0][:, 0:3], ALU.mult).then_inc(sem("rtok_ready"), 1)

        @block.gpsimd
        def _(pool):
            own = Own(pool, sem("pool_own"))

            def copy(out, a, by=None):
                one = ones[:, 0:1] if by is None else by
                for k in range(len(out.shape) - 2):
                    one = one.unsqueeze(1)
                return pool.tensor_tensor(out, a, one.broadcast_to(list(out.shape)), ALU.mult)

            own.link(pool.memset(ident[:, :], 0.0))
            pool.affine_select(out=ident[:, :], in_=ident[:, :], compare_op=ALU.not_equal, fill=1.0, base=0, pattern=[[-1, P]],
                               channel_multiplier=1).then_inc(sem("consts_ready"), 1)
            pool.wait_ge(sem("consts_ready"), 1)
            own.link(pool.memset(rtok[:, :], 1.0))
            pool.memset(ones[:, :], 1.0).then_inc(sem("consts_ready"), 1)
            pool.wait_ge(sem("consts_ready"), 2)
            for j in range(3):
                pool.dma_start(cvn[:, j, :], I["conv_w"][j].rearrange("(t p) -> t p", p=P)).then_inc(sem("cv_in"), 16)
            pool.dma_start(cvn[:, 3, :], I["conv_b"].rearrange("(t p) -> t p", p=P)).then_inc(sem("cv_in"), 16)
            pool.dma_start(lsn[64:96, :], I["s5_log_step"].rearrange("(i g) -> i g", g=2)).then_inc(sem("ls_in"), 16)
            pool.dma_start(apn[0:NPAIR, :], I["s5_a_re"].rearrange("(i g) p -> i (g p)", g=2)).then_inc(sem("ap_in"), 16)
            pool.dma_start(apn[NPAIR:2 * NPAIR, :], I["s5_a_im"].rearrange("(i g) p -> i (g p)", g=2)).then_inc(sem("ap_in"), 16)
            for c, n in enumerate(("re", "im")):
                pool.dma_start(stn[:, c, :, :], I[f"state_s5_{n}"].rearrange("(h b) (i g) p -> (b i) h (g p)", h=2, g=2)).then_inc(sem("st_in"), 16)
                pool.dma_start(bnat[:, c, :, :], I[f"s5_b_{n}"].rearrange("(i g) p c -> (g p) i c", g=2)).then_inc(sem("bn_in"), 16)
                pool.dma_start(cnat[:, c, :, :], I[f"s5_c_{n}"].rearrange("(j g) c p -> (g c) j p", g=8)).then_inc(sem("cn_in"), 16)
            pool.dma_start(ptab[:, :], I["page_table"].rearrange("(o b) g -> o (b g)", o=1)).then_inc(sem("pt_in"), 16)
            pool.wait_ge(sem("ls_in"), 16)
            pool.tensor_copy(apn[64:96, :].rearrange("i (g p) -> i g p", g=2), bc(lsn[64:96, :], 2, NST)).then_inc(sem("lstep_wide"), 1)
            pool.wait_ge(sem("lstep_wide"), 1)
            own.link(pool.memset(m3[:, :, :], 0.0))
            pool.affine_select(out=m3[:, :, :].rearrange("p h (b t) -> p h b t", b=4), in_=m3[:, :, :].rearrange("p h (b t) -> p h b t", b=4),
                               compare_op=ALU.not_equal, fill=1.0, base=0, pattern=[[-4, 8], [-32, 4], [-1, 4]],
                               channel_multiplier=1).then_inc(sem("m3_ready"), 1)
            pool.wait_ge(sem("m3_ready"), 1)
            own.link(pool.memset(reset[:, :], 1.0))
            own.link(pool.memset(reset[:, TP:T].rearrange("p (b t) -> p b t", b=NB)[:, :, 0:1], 0.0))
            for k, s in ((0, 1), (1, 16)):
                own.link(pool.iota(nramp[:, 16 * k:16 * k + 16], pattern=[[s, 16]], base=0, channel_multiplier=0, allow_small_or_imprecise_dtypes=True))
            own.link(pool.memset(half[:, :], 0.0))
            for n in range(2):
                own.link(pool.memset(half[DH * n:DH * (n + 1), n:n + 1], 1.0))
            for t in (e1, e1r, e2):
                own.link(pool.memset(t[:, NPAIR, :, :], 0.0))
            pool.wait_ge(sem("pt_in"), 16)
            pool.wait_ge(sem("ss_ready"), 3)
            pool.wait_ge(sem("xt_ready"), KD)
            with loop("Pool", 0, NB * NPAGES) as i:
                page = pool.value_load(ptab[0:1, ds(i, 1)], min_val=0, max_val=NPOOL - 1)
                pool.dma_start(kidx[:, ds(i, 1), :], I["cache_kidx"][ds(page, 1)].rearrange("a p d -> p a d")).then_inc(sem("kidx_in"), 16)

            def ts(out, a, s1, s2, o1, o2):
                own.link(pool.tensor_scalar(out, a, s1, s2, o1, o2))

            def tt(out, a, b, op):
                own.link(pool.tensor_tensor(out, a, b, op))

            def stt(out, a, s, b, o1, o2, via=None):
                ts(out if via is None else via, a, s, None, o1, ALU.bypass)
                tt(out, out if via is None else via, b, o2)

            def exp(out, x, y, f):
                ts(y, x, LOG2E, MAGIC, ALU.mult, ALU.add)
                ts(y, y, -MAGIC, -126.0, ALU.add, ALU.max)
                ts(y, y, 127.0, None, ALU.min, ALU.bypass)
                stt(f, y, -LN2H, x, ALU.mult, ALU.add)
                stt(f, y, -LN2L, f, ALU.mult, ALU.add, via_[:, :])
                ts(out, f, 1.0 / 40320.0, None, ALU.mult, ALU.bypass)
                for k in (5040.0, 720.0, 120.0, 24.0, 6.0, 2.0, 1.0):
                    stt(out, out, 1.0 / k, f, ALU.add, ALU.mult)
                ts(smi[:, :], y, 127.0, 8388608.0, ALU.add, ALU.mult)
                stt(out, out, 1.0, smi[:, :].bitcast(F32), ALU.add, ALU.mult)

            pool.wait_ge(sem("par_ready"), 3)
            are, aim, lst = params[:, 0:32], params[:, 32:64], params[:, 64:96]
            step, xr, th, k_, lr, li, fr, fi, den, nr, ni, u1, u2, y_, f_ = (sm[i][:, :] for i in range(15))
            tt(den, are, are, ALU.mult)
            tt(u1, aim, aim, ALU.mult)
            pool.tensor_tensor(den, den, u1, ALU.add).then_inc(sem("den_sum"), 1)
            exp(step, lst, y_, f_)
            tt(xr, are, step, ALU.mult)
            exp(rdec[:, :], xr, y_, f_)
            tt(th, aim, step, ALU.mult)
            ts(k_, th, 1.0 / TWO_PI, MAGIC, ALU.mult, ALU.add)
            ts(k_, k_, -MAGIC, None, ALU.add, ALU.bypass)
            for c in (PI1, PI2, PI3):
                stt(th, k_, -c, th, ALU.mult, ALU.add, via_[:, :])
            own.link(pool.tensor_copy(ang_hi[:, :], th))
            own.link(pool.tensor_copy(u1, ang_hi[:, :]))
            tt(u2, th, u1, ALU.subtract)
            ramp = bc(nramp[:, :], 1, NPAIR)
            a0, a1, a2, a3 = (t[:, :, :] for t in tmp)
            tt(a0, bc(u1, 2, 32), ramp, ALU.mult)
            tt(a1, bc(u2, 2, 32), ramp, ALU.mult)
            tt(a2, a0, a1, ALU.add)
            ts(a3, a2, 1.0 / TWO_PI, MAGIC, ALU.mult, ALU.add)
            ts(a3, a3, -MAGIC, None, ALU.add, ALU.bypass)
            stt(a0, a3, -PI1, a0, ALU.mult, ALU.add, a2)
            tt(a0, a0, a1, ALU.add)
            stt(a0, a3, -PI2, a0, ALU.mult, ALU.add, a2)
            stt(a2, a3, -PI3, a0, ALU.mult, ALU.add)
            ts(a2, a2, -PI_IN, PI_IN, ALU.max, ALU.min)
            ts(a3, a2, TWO_PI / 4, -TWO_PI, ALU.is_gt, ALU.mult)
            stt(a3, a2, TWO_PI / 4, a3, ALU.add, ALU.add, a0)
            pool.tensor_scalar(a3, a3, -PI_IN, PI_IN, ALU.max, ALU.min).then_inc(sem("angles_ready"), 1)
            pool.wait_ge(sem("cn_in"), 32)
            pool.wait_ge(sem("parity_ready"), 1)
            for c in range(2):
                for g in range(2):
                    ts(cdg[:, c, :, NST * g:NST * (g + 1)], cnat[:, c, :, :], parity[:, 2 * c + g:2 * c + g + 1], None, ALU.mult, ALU.bypass)
            pool.memset(bdg[:, :, :, :], 0.0).then_inc(sem("cdg_ready"), 1)
            pool.wait_ge(sem("cdg_ready"), 1)
            pool.wait_ge(sem("sines_ready"), 6)
            tt(lr, rdec[:, :], e2[:, 0:NPAIR, 0, 1], ALU.mult)
            tt(li, rdec[:, :], e2[:, 0:NPAIR, 1, 1], ALU.mult)
            ts(nr, lr, -1.0, None, ALU.add, ALU.bypass)
            pool.wait_ge(sem("den_ready"), 1)
            for out, (p1, q1), (p2, q2), op in ((fr, (nr, are), (li, aim), ALU.add), (fi, (li, are), (nr, aim), ALU.subtract)):
                tt(u1, p1, q1, ALU.mult)
                tt(u2, p2, q2, ALU.mult)
                tt(u1, u1, u2, op)
                tt(out, u1, den, ALU.mult)
            pool.wait_ge(sem("bn_in"), 32)
            b1, b2 = tmp[0][:, :, 0:GC], tmp[1][:, :, 0:GC]
            for c, (x, y, op) in enumerate(((0, 1, ALU.subtract), (1, 0, ALU.add))):
                tt(b1, bc(fr, 2, GC), bnat[:, x, :, :], ALU.mult)
                tt(b2, bc(fi, 2, GC), bnat[:, y, :, :], ALU.mult)
                for g in range(2):
                    r = slice(NST * g, NST * (g + 1))
                    tt(bdg[r, c, :, GC * g:GC * (g + 1)], b1[r], b2[r], op)
            v1 = tmp[2][:, 0:8, :]
            v2 = tmp[3][:, 0:8, :]
            for c, (x, y, op) in enumerate(((0, 1, ALU.subtract), (1, 0, ALU.add))):
                tt(v1, bc(lr, 1, NB), x0[:, x, :, :], ALU.mult)
                tt(v2, bc(li, 1, NB), x0[:, y, :, :], ALU.mult)
                tt(inj[:, c, :, :].rearrange("p i b -> p b i"), v1, v2, op)
            pool.memset(u1, 0.0).then_inc(sem("bc_ready"), 1)
            pool.wait_ge(sem("bc_ready"), 1)

            for b in range(2):
                if b:
                    pool.wait_ge(sem("sc_masked"), b)
                pool.wait_ge(sem("isc_sum"), b + 1)
                pool.affine_select(out=sc[b][:, :], in_=sc[b][:, :], compare_op=ALU.is_ge, fill=NEG, base=P * b,
                                   pattern=[[-1, P * (b + 1)]], channel_multiplier=1).then_inc(sem("sc_masked"), 1)

            def angles(pr, i):
                t = tab[i % 2]

                def e(tile, c=None):
                    a = tile[:, ds(pr, 1), :, :].rearrange("p o c a -> p (o c) a")
                    return a if c is None else a[:, c, :]
                grid = t[:, :, 0:TP].rearrange("p c (a b) -> p c a b", a=16)
                pool.tensor_tensor(tqs[i % 2][:, :, :, :], bc(e(e1), 3, 16), bc(bc(e(e2, 0), 1, 16), 1, 2), ALU.mult).then_inc(sem("tab_ready"), 1)
                pool.tensor_tensor(grid, bc(e(e1r), 3, 16), bc(bc(e(e2, 1), 1, 16), 1, 2), ALU.mult).then_inc(sem("tab_ready"), 1)
                copy(t[:, :, TP:T].rearrange("p c (b t) -> p c b t", b=NB), bc(e(e2)[:, :, 0:DS], 2, NB)).then_inc(sem("tab_ready"), 1)

            def turn_forward(it, i):
                pool.wait_ge(sem("ws_ready"), 4 * it + i + 1)
                w, x, c, s = ws[i % 2], xs[i], tab[i % 2][:, 0, :], tab[i % 2][:, 1, :]
                own(pool.tensor_tensor(x[:, :, :], w[:, :, :], bc(c, 1, 2), ALU.mult))
                own.link(pool.tensor_tensor(xb[:, :, :], w[:, :, :], bc(s, 1, 2), ALU.mult))
                pool.tensor_tensor(x[:, 0, :], x[:, 0, :], xb[:, 1, :], ALU.subtract).then_inc(sem("xs_ready"), 1)
                pool.tensor_tensor(x[:, 1, :], x[:, 1, :], xb[:, 0, :], ALU.add).then_inc(sem("xs_ready"), 1)
                pool.wait_ge(sem("xs_ready"), 8 * it + 2 * i + 2)
                pr = 4 * it + i
                copy(last[:, :, 8:9, ds(pr, 1)].rearrange("p c k o -> p c (k o)"), x[:, :, TP - 1:TP]).then_inc(sem("last_ready"), 1)
                copy(last[:, :, 0:NB, ds(pr, 1)].rearrange("p c b o -> p c (b o)"),
                     x[:, :, TP:T].rearrange("p c (b t) -> p c b t", b=NB)[:, :, :, DS - 1]).then_inc(sem("last_ready"), 1)
                pool.wait_ge(sem("last_ready"), 2 * pr + 2)

            def states(it, first=False):
                for i in range(4):
                    angles(4 * it + i + 1, i + 1)
                    if i == 0 and not first:
                        pool.wait_ge(sem("y_ready"), it)
                    turn_forward(it, i)

            pool.wait_ge(sem("ssc_t"), 1)
            pool.wait_ge(sem("bct_ready"), 8)
            angles(0, 0)
            states(0, first=True)
            with loop("Pool", 1, N_GATE) as it:
                own.loop(it - 1, 8)
                states(it)
            own.done(N_GATE - 1)
            def stage_unit(i, j):
                copy(qs[:, :], qT[:, ds(i, 1), :].rearrange("p o t -> p (o t)")).then_inc(sem("unit_staged"), 1)
                copy(ks[:, :], kT[:, ds(j, 1), :].rearrange("p o t -> p (o t)")).then_inc(sem("unit_staged"), 1)
                copy(vs[:, :, :], vtok[:, :, ds(P * j, P)]).then_inc(sem("unit_staged"), 1)
                for n in range(2):
                    copy(qbs[:, :, 16 * n:16 * (n + 1)].rearrange("p a (g t) -> p a g t", g=4), sample_cols(qT, slice(0, P), i),
                         half[:, n:n + 1]).then_inc(sem("new_ready"), 1)
                copy(kTb[:, :, PAST:SK], kT[:, :, ds(TP + DS * i, DS)]).then_inc(sem("new_ready"), 1)

            stage_unit(0, 0)
            for par in range(2):
                pool.wait_ge(sem(f"gates_out{par}"), 16 * (N_GATE + 1 - par))
            pool.dma_start(ga[:, :, :], W["gates"][0:KD].rearrange("a p t -> p a t")).then_inc(sem("ga_in"), 16)
            pool.wait_ge(sem("masks_ready"), 1)
            pool.dma_start(W["mask"], wk[2][:, :]).then_inc(sem("mask_out"), 16)
            pool.memset(gbt[:, :, :], 0.0).then_inc(sem("glu_free"), 1)
            pool.wait_ge(sem("glu_free"), 1)

            def gate_branch(i):
                pool.dma_start(gbt[:, :, :], W["gates"][ds(KD + 2 * i, 2)].rearrange("a p t -> p a t")).then_inc(sem("gb_in"), 16)
                pool.wait_ge(acc_free[0], 16 + i)
                pool.wait_ge(sem("gb_in"), 16 * i + 16)
                pool.tensor_tensor(yb[:, ds(2 * i, 2), :], glu_a[:, :, :], gbt[:, :, :], ALU.mult).then_inc(sem("glu_free"), 1)
                pool.wait_ge(sem("glu_free"), i + 2)

            with loop("Pool", 0, 7) as i:
                for used in ("s_ready", "ss_t", "o_ready"):
                    pool.wait_ge(sem(used), i + 1)
                stage_unit(i + 1, (i + 1) // 4)
                gate_branch(i)
            gate_branch(7)
            own.link(pool.memset(sqacc[:, :], 0.0))

            def squares(x, tile, buf, done):
                own.link(pool.tensor_tensor(buf[:, :, :], x[:, ds(tile, 2), :], x[:, ds(tile, 2), :], ALU.mult))
                own.link(pool.tensor_tensor(sqacc[:, :], sqacc[:, :], buf[:, 0, :], ALU.add))
                pool.tensor_tensor(sqacc[:, :], sqacc[:, :], buf[:, 1, :], ALU.add).then_inc(sem("sq_done"), 1)
                pool.wait_ge(sem("sq_done"), done)

            with loop("Pool", 0, N_OUT) as it:
                own.loop(it, 4)
                for s in range(2):
                    pool.wait_ge(acc_free[1 - s], 27 + it + s)
                    squares(x2, 4 * it + 2 * s, sq2, 2 * it + s + 1)
            own.done(N_OUT)
            pool.wait_ge(sem("sum_ready"), 1)
            own.link(pool.memset(sqacc[:, :], 0.0))
            pool.wait_ge(sem("cst_ready"), 3)
            pool.memset(up[:, :, 0:2], 0.0).then_inc(sem("cst_saved"), 1)
            pool.wait_ge(sem("cst_saved"), 1)

            with loop("Pool", 0, N_UP) as it:
                own.loop(it, 4)
                pool.wait_ge(lo_ready, C_UP + 8 * it + 4)
                for k in range(4):
                    t = KF * (k // 2) + k % 2
                    ins = copy(up[:, k, 2 + TP:LU].rearrange("p (b t) -> p b t", b=NB)[:, :, 0:2],
                                             cstate[:, ds(t + 2 * it, 1), 0:16].rearrange("p o (b t) -> p (o b) t", b=NB))
                    if k < 3:
                        own.link(ins)
                    else:
                        ins.then_inc(sem("cst_in_up"), 1)
                pool.wait_ge(sem("cst_in_up"), it + 1)
                pool.wait_ge(acc_free[0], 32 + it)
                own(copy(rtok[:, 7:8], ones[:, 0:1]))
                for h in (1, 0):
                    copy(cstate[:, ds(KF * h + 2 * it, 2), :].rearrange("p a (k s) -> p a k s", k=9), new_states(h)).then_inc(sem("cst_saved"), 1)
                pool.wait_ge(sem("cst_saved"), 2 * it + 3)
            own.done(N_UP)
            pool.wait_ge(sem("crow_ready"), 4)
            rows = O["conv_state"].rearrange("r (t p) -> r t p", p=P)
            for t in range(7):
                pool.dma_start(rows[:, 0:84, :].rearrange("r (k t) p -> r k t p", t=7)[:, :, t, :], cnat_out[18 * t:18 * t + 18, 0:12, :]
                               ).then_inc(sem("crow_stored"), 16)
            for t in range(4):
                pool.dma_start(rows[:, 84 + t, :], cnat_out[18 * t:18 * t + 18, 12, :]).then_inc(sem("crow_stored"), 16)
            with loop("Pool", 0, 4) as it:
                own.loop(it, 4)
                for s in range(2):
                    pool.wait_ge(acc_free[1 - s], 53 + it + s)
                    squares(x3, 4 * it + 2 * s, sq3, 9 + 2 * it + s)
            own.done(4)


_OUTS = {
    "y_prompt": (TP, D), "y_sample": (TS, D), "k_prompt": (TP, KV), "v_prompt": (TP, KV), "kidx_prompt": (TP, DI),
    "s5_state": (2, 9, NPAIR, P), "conv_state": (2 + 2 * NB, 2 * FF), "k_sample": (TS, KV), "v_sample": (TS, KV), "kidx_sample": (TS, DI),
}
_SCRATCH = {"x_kept": (P, KD * T), "wi": (4, IH, DS, 2), "gates": (32, P, T), "mask": (TS, SK)}


def build(nc, shapes):
    ins = {n: nc.dram_tensor(f"in_{n}", s, mybir.dt.from_np(t), kind="ExternalInput").ap() for n, (s, t) in shapes.items()}
    outs = {n: nc.dram_tensor(f"out_{n}", s, F32, kind="ExternalOutput").ap() for n, s in _OUTS.items()}
    scratch = {n: nc.dram_tensor(f"scratch_{n}", s, F32).ap() for n, s in _SCRATCH.items()}
    hybrid_decoder_step_kernel(nc, ins, outs, scratch)


def kernel(**inputs):
    import numpy as np
    import concourse.bacc as bacc
    from concourse.bass_utils import run_bass_kernel_spmd

    arrays = {}
    for n, a in inputs.items():
        a = np.ascontiguousarray(a)
        if n in ("x_prompt", "x_sample"):
            a = a.reshape(-1, D)
        elif n not in ("page_table", "norm_final"):
            a = a[0]
            if n in ("cache_k", "cache_v"):
                a = a.reshape(NPOOL, PAGE, KV)
        arrays[n] = a
    nc = bacc.Bacc("TRN2", target_bir_lowering=False, num_devices=1)
    build(nc, {n: (a.shape, a.dtype) for n, a in arrays.items()})
    r = run_bass_kernel_spmd(nc, [{f"in_{n}": a for n, a in arrays.items()}], core_ids=[0]).results[0]
    o = {n: r[f"out_{n}"] for n in _OUTS}
    s5 = o["s5_state"].reshape(2, 9, GRP, NST)
    conv = o["conv_state"]
    return (o["y_prompt"].reshape(1, TP, D), o["y_sample"].reshape(NB, DS, D),
            o["k_prompt"].reshape(1, 1, TP, NKV, DH), o["v_prompt"].reshape(1, 1, TP, NKV, DH), o["kidx_prompt"].reshape(1, 1, TP, DI),
            s5[0, 8].reshape(1, 1, GRP, NST), s5[1, 8].reshape(1, 1, GRP, NST), conv[0:2].reshape(1, 1, 2, 2 * FF),
            o["k_sample"].reshape(1, NB, DS, NKV, DH), o["v_sample"].reshape(1, NB, DS, NKV, DH), o["kidx_sample"].reshape(1, NB, DS, DI),
            s5[0, 0:8].reshape(1, NB, GRP, NST), s5[1, 0:8].reshape(1, NB, GRP, NST), conv[2:].reshape(1, NB, 2, 2 * FF))
```
